# Optimizing a Trainium2 kernel written in Bass

```python
import jax, jax.numpy as jnp
from jax import lax
import numpy as np

D_MODEL = 1024
BATCH = 1
SEQ = 256
DEPTH = 1
DEC_BATCH = 8
DEC_SEQ = 8
PAST_LEN = 1024
PAGE_SIZE = 128

SWA_HEADS = 8
SWA_KV_HEADS = 2
SWA_HEAD_DIM = 64
SWA_GROUP = SWA_HEADS // SWA_KV_HEADS
WINDOW = 128
SWA_BLOCK = 128
ATTN_SCALE = SWA_HEAD_DIM ** -0.5
GLA_HEADS = 4
GLA_DK = 64
GLA_DV = 128
GLA_GATE_RANK = 16
GLA_GATE_NORM = 16.0
GLA_CHUNK = 16
GLA_SCALE = GLA_DK ** -0.5
A_WIDTH = SWA_HEADS * SWA_HEAD_DIM
KV_WIDTH = SWA_KV_HEADS * SWA_HEAD_DIM
GLA_K_WIDTH = GLA_HEADS * GLA_DK
B_WIDTH = GLA_HEADS * GLA_DV
IN_SPLITS = (A_WIDTH, KV_WIDTH, KV_WIDTH, GLA_K_WIDTH, GLA_K_WIDTH, B_WIDTH, GLA_GATE_RANK, B_WIDTH, D_MODEL, D_MODEL)
IN_WIDTH = sum(IN_SPLITS)
N_EXPERTS = 32
TOP_K = 4
D_FF = D_MODEL
SWIGLU_ALPHA = 1.702
SWIGLU_LIMIT = 7.0
MOE_BLOCK = 128
NORM_EPS = 1e-5
QK_EPS = 1e-6
NEG_INF = -1e30

kernel_name = "hybrid_swa_sink_gla_moe_step"

def rmsnorm(x, g, eps):
    xf = x.astype(jnp.float32)
    y = xf * lax.rsqrt(jnp.mean(xf * xf, axis=-1, keepdims=True) + eps)
    return (y * g.astype(jnp.float32)).astype(x.dtype)

def mixer_inputs(x, norm1, w_in, q_norm, k_norm, w_gk, b_gk):
    lead = x.shape[:-1]
    u = rmsnorm(x, norm1, NORM_EPS) @ w_in
    offsets = np.cumsum(IN_SPLITS)[:-1].tolist()
    qa, ka, va, qb, kb, vb, g_low, r_b, g_a, g_b = jnp.split(u, offsets, axis=-1)
    qa = rmsnorm(qa.reshape(*lead, SWA_HEADS, SWA_HEAD_DIM), q_norm, QK_EPS)
    ka = rmsnorm(ka.reshape(*lead, SWA_KV_HEADS, SWA_HEAD_DIM), k_norm, QK_EPS)
    va = va.reshape(*lead, SWA_KV_HEADS, SWA_HEAD_DIM)
    qb = qb.reshape(*lead, GLA_HEADS, GLA_DK) * GLA_SCALE
    kb = kb.reshape(*lead, GLA_HEADS, GLA_DK)
    vb = vb.reshape(*lead, GLA_HEADS, GLA_DV)
    log_a = (jax.nn.log_sigmoid((g_low @ w_gk + b_gk).astype(jnp.float32)) / GLA_GATE_NORM).reshape(*lead, GLA_HEADS, GLA_DK)
    return qa, ka, va, qb, kb, vb, log_a, r_b, g_a, g_b

def attend_with_sinks(s, v, sinks, eq):
    sink = sinks.astype(jnp.float32).reshape(SWA_KV_HEADS, SWA_GROUP, 1, 1)
    sink = jnp.broadcast_to(sink, s.shape[:-1] + (1,))
    p = jax.nn.softmax(jnp.concatenate([s, sink], axis=-1), axis=-1)[..., :-1]
    return jnp.einsum(eq, p.astype(v.dtype), v)

def swa_prompt(q, k, v, sinks):
    bsz, L = q.shape[:2]
    nb = L // SWA_BLOCK
    qb = q.reshape(bsz, nb, SWA_BLOCK, SWA_KV_HEADS, SWA_GROUP, SWA_HEAD_DIM)

    def band(t):
        tb = t.reshape(bsz, nb, SWA_BLOCK, SWA_KV_HEADS, SWA_HEAD_DIM)
        prev = jnp.pad(tb, ((0, 0), (1, 0), (0, 0), (0, 0), (0, 0)))[:, :-1]
        return jnp.concatenate([prev, tb], axis=2)

    kb, vb = band(k), band(v)
    s = jnp.einsum('bnqkgd,bnckd->bnkgqc', qb, kb, preferred_element_type=jnp.float32) * ATTN_SCALE
    qi = jnp.arange(SWA_BLOCK)[:, None]
    ci = jnp.arange(2 * SWA_BLOCK)[None, :]
    dist = SWA_BLOCK + qi - ci
    band_mask = (dist >= 0) & (dist < WINDOW)
    key_pos = jnp.arange(nb)[:, None, None] * SWA_BLOCK + ci[None] - SWA_BLOCK
    mask = band_mask[None] & (key_pos >= 0)
    s = jnp.where(mask[None, :, None, None], s, NEG_INF)
    o = attend_with_sinks(s, vb, sinks, 'bnkgqc,bnckd->bnqkgd')
    return o.reshape(bsz, L, A_WIDTH)

def swa_sample(q, k, v, cache_k, cache_v, sinks):
    bsz, L = q.shape[:2]
    w = cache_k.shape[1]
    keys = jnp.concatenate([cache_k.astype(k.dtype), k], axis=1)
    vals = jnp.concatenate([cache_v.astype(v.dtype), v], axis=1)
    qg = q.reshape(bsz, L, SWA_KV_HEADS, SWA_GROUP, SWA_HEAD_DIM)
    s = jnp.einsum('bqkgd,bckd->bkgqc', qg, keys, preferred_element_type=jnp.float32) * ATTN_SCALE
    dist = w + jnp.arange(L)[:, None] - jnp.arange(w + L)[None, :]
    mask = (dist >= 0) & (dist < WINDOW)
    s = jnp.where(mask, s, NEG_INF)
    o = attend_with_sinks(s, vals, sinks, 'bkgqc,bckd->bqkgd').reshape(bsz, L, A_WIDTH)
    return o, keys[:, -w:], vals[:, -w:]

def gla_chunked(q, k, v, log_a, s0):
    out_dtype = v.dtype
    bsz, L, nh, dk = q.shape
    dv = v.shape[-1]
    c = GLA_CHUNK if L % GLA_CHUNK == 0 else L
    n = L // c

    def chunks(t):
        t = t.astype(jnp.float32)
        return jnp.moveaxis(t.reshape(bsz, n, c, *t.shape[2:]), 1, 0)

    causal = jnp.tril(jnp.ones((c, c), dtype=bool))[None, :, :, None, None]

    def step(s, inp):
        qc, kc, vc, gc = inp
        b = jnp.cumsum(gc, axis=1)
        o_inter = jnp.einsum('bthk,bhkv->bthv', qc * jnp.exp(b), s)
        rel = jnp.where(causal, b[:, :, None] - b[:, None, :], -jnp.inf)
        a = jnp.einsum('bthk,btshk,bshk->bhts', qc, jnp.exp(rel), kc)
        o_intra = jnp.einsum('bhts,bshv->bthv', a, vc)
        b_last = b[:, -1]
        s_new = jnp.exp(b_last)[..., None] * s + jnp.einsum('bshk,bshv->bhkv', kc * jnp.exp(b_last[:, None] - b), vc)
        return s_new, o_inter + o_intra

    s_final, o = lax.scan(step, s0.astype(jnp.float32), (chunks(q), chunks(k), chunks(v), chunks(log_a)))
    o = jnp.moveaxis(o, 0, 1).reshape(bsz, L, nh, dv)
    return o.astype(out_dtype), s_final

def expert_mlp(x, w1, b1, w2, b2):
    u = x @ w1 + b1
    x_glu = jnp.minimum(u[..., ::2], SWIGLU_LIMIT)
    x_lin = jnp.clip(u[..., 1::2], -SWIGLU_LIMIT, SWIGLU_LIMIT)
    return (x_glu * jax.nn.sigmoid(SWIGLU_ALPHA * x_glu) * (x_lin + 1.0)) @ w2 + b2

def moe(h, w_router, b_router, w1, b1, w2, b2):
    lead = h.shape[:-1]
    x2 = h.reshape(-1, D_MODEL)
    T = x2.shape[0]
    logits = jnp.dot(x2, w_router, preferred_element_type=jnp.float32) + b_router.astype(jnp.float32)
    top_v, top_e = lax.top_k(logits, TOP_K)
    gate = jax.nn.softmax(top_v, axis=-1)
    flat_e = top_e.reshape(-1).astype(jnp.int32)
    flat_t = jnp.repeat(jnp.arange(T, dtype=jnp.int32), TOP_K)
    flat_g = gate.reshape(-1)
    order = jnp.argsort(flat_e)
    se = flat_e[order]
    counts = jnp.bincount(flat_e, length=N_EXPERTS).astype(jnp.int32)
    padded = (counts + MOE_BLOCK - 1) // MOE_BLOCK * MOE_BLOCK
    pad_end = jnp.cumsum(padded)
    pad_start = pad_end - padded
    start = jnp.cumsum(counts) - counts
    dest = pad_start[se] + jnp.arange(T * TOP_K, dtype=jnp.int32) - start[se]
    n_rows = -(-(T * TOP_K + N_EXPERTS * (MOE_BLOCK - 1)) // MOE_BLOCK) * MOE_BLOCK
    n_blocks = n_rows // MOE_BLOCK
    row_tok = jnp.full((n_rows,), T, jnp.int32).at[dest].set(flat_t[order])
    row_g = jnp.zeros((n_rows,), jnp.float32).at[dest].set(flat_g[order])
    blk_e = jnp.minimum(jnp.searchsorted(pad_end, jnp.arange(n_blocks, dtype=jnp.int32) * MOE_BLOCK, side='right'), N_EXPERTS - 1)
    x_pad = jnp.concatenate([x2, jnp.zeros((1, D_MODEL), x2.dtype)], axis=0)
    xb = x_pad[row_tok].reshape(n_blocks, MOE_BLOCK, D_MODEL)

    def expert_block(args):
        xe, e = args
        return expert_mlp(xe, w1[e], b1[e], w2[e], b2[e])

    yb = lax.map(expert_block, (xb, blk_e)).reshape(n_rows, D_MODEL)
    y = jax.ops.segment_sum(yb.astype(jnp.float32) * row_g[:, None], row_tok, num_segments=T + 1)[:T]
    return y.astype(h.dtype).reshape(*lead, D_MODEL)

def block_output(x, oa, ob, r_b, g_a, g_b, gla_norm, w_a, w_b, w_o, norm2, w_router, b_router, w1, b1, w2, b2):
    ob = rmsnorm(ob, gla_norm, NORM_EPS).reshape(*x.shape[:-1], B_WIDTH) * jax.nn.silu(r_b)
    merged = jax.nn.sigmoid(g_a) * (oa @ w_a) + jax.nn.sigmoid(g_b) * (ob @ w_b)
    h = x + merged @ w_o
    return h + moe(rmsnorm(h, norm2, NORM_EPS), w_router, b_router, w1, b1, w2, b2)

def decoder_layer(x_p, x_s, cache_k, cache_v, s_gla, norm1, w_in, q_norm, k_norm, sinks, w_gk, b_gk,
                  gla_norm, w_a, w_b, w_o, norm2, w_router, b_router, w1, b1, w2, b2):
    mix_w = (norm1, w_in, q_norm, k_norm, w_gk, b_gk)
    out_w = (gla_norm, w_a, w_b, w_o, norm2, w_router, b_router, w1, b1, w2, b2)
    qa, ka, va, qb, kb, vb, la, rb, ga, gb = mixer_inputs(x_p, *mix_w)
    oa = swa_prompt(qa, ka, va, sinks)
    s0 = jnp.zeros((x_p.shape[0], GLA_HEADS, GLA_DK, GLA_DV), jnp.float32)
    ob, s_p = gla_chunked(qb, kb, vb, la, s0)
    y_p = block_output(x_p, oa, ob, rb, ga, gb, *out_w)
    k_p, v_p = ka[:, -WINDOW:], va[:, -WINDOW:]
    qa, ka, va, qb, kb, vb, la, rb, ga, gb = mixer_inputs(x_s, *mix_w)
    oa, k_s, v_s = swa_sample(qa, ka, va, cache_k, cache_v, sinks)
    ob, s_s = gla_chunked(qb, kb, vb, la, s_gla)
    y_s = block_output(x_s, oa, ob, rb, ga, gb, *out_w)
    return y_p, y_s, (k_p, v_p, s_p, k_s, v_s, s_s)

def setup_inputs(seed: int = 0) -> dict:
    key = jax.random.key(seed)
    ks = jax.random.split(key, 32)

    def nrm(k, shape, scale):
        return jax.random.normal(k, shape, jnp.float32) * scale

    win = min(WINDOW, PAST_LEN)
    return {
        "x_prompt": nrm(ks[0], (BATCH, SEQ, D_MODEL), 1.0),
        "x_sample": nrm(ks[1], (DEC_BATCH, DEC_SEQ, D_MODEL), 1.0),
        "cache_swa_k": nrm(ks[2], (DEPTH, DEC_BATCH, win, SWA_KV_HEADS, SWA_HEAD_DIM), 1.0),
        "cache_swa_v": nrm(ks[3], (DEPTH, DEC_BATCH, win, SWA_KV_HEADS, SWA_HEAD_DIM), 1.0),
        "state_gla": nrm(ks[4], (DEPTH, DEC_BATCH, GLA_HEADS, GLA_DK, GLA_DV), 1.0),
        "norm1": 1.0 + nrm(ks[5], (DEPTH, D_MODEL), 0.01),
        "w_in": nrm(ks[6], (DEPTH, D_MODEL, IN_WIDTH), D_MODEL ** -0.5),
        "q_norm": 1.0 + nrm(ks[7], (DEPTH, SWA_HEAD_DIM), 0.01),
        "k_norm": 1.0 + nrm(ks[8], (DEPTH, SWA_HEAD_DIM), 0.01),
        "sinks": nrm(ks[9], (DEPTH, SWA_HEADS), 0.5),
        "w_gk": nrm(ks[10], (DEPTH, GLA_GATE_RANK, GLA_K_WIDTH), GLA_GATE_RANK ** -0.5),
        "b_gk": nrm(ks[11], (DEPTH, GLA_K_WIDTH), 0.01),
        "gla_norm": 1.0 + nrm(ks[12], (DEPTH, GLA_DV), 0.01),
        "w_a": nrm(ks[13], (DEPTH, A_WIDTH, D_MODEL), A_WIDTH ** -0.5),
        "w_b": nrm(ks[14], (DEPTH, B_WIDTH, D_MODEL), B_WIDTH ** -0.5),
        "w_o": nrm(ks[15], (DEPTH, D_MODEL, D_MODEL), D_MODEL ** -0.5),
        "norm2": 1.0 + nrm(ks[16], (DEPTH, D_MODEL), 0.01),
        "w_router": nrm(ks[17], (DEPTH, D_MODEL, N_EXPERTS), D_MODEL ** -0.5),
        "b_router": nrm(ks[18], (DEPTH, N_EXPERTS), 0.01),
        "w1": nrm(ks[19], (DEPTH, N_EXPERTS, D_MODEL, 2 * D_FF), D_MODEL ** -0.5),
        "b1": nrm(ks[20], (DEPTH, N_EXPERTS, 2 * D_FF), 0.01),
        "w2": nrm(ks[21], (DEPTH, N_EXPERTS, D_FF, D_MODEL), D_FF ** -0.5),
        "b2": nrm(ks[22], (DEPTH, N_EXPERTS, D_MODEL), 0.01),
    }

def reference(x_prompt, x_sample, cache_swa_k, cache_swa_v, state_gla, norm1, w_in, q_norm, k_norm, sinks,
              w_gk, b_gk, gla_norm, w_a, w_b, w_o, norm2, w_router, b_router, w1, b1, w2, b2):
    y_p, y_s = x_prompt, x_sample
    states = []
    for l in range(DEPTH):
        y_p, y_s, st = decoder_layer(
            y_p, y_s, cache_swa_k[l], cache_swa_v[l], state_gla[l],
            norm1[l], w_in[l], q_norm[l], k_norm[l], sinks[l], w_gk[l], b_gk[l],
            gla_norm[l], w_a[l], w_b[l], w_o[l], norm2[l], w_router[l], b_router[l],
            w1[l], b1[l], w2[l], b2[l])
        states.append(st)
    swa_k_prompt = jnp.stack([st[0] for st in states])
    swa_v_prompt = jnp.stack([st[1] for st in states])
    gla_state_prompt = jnp.stack([st[2] for st in states])
    swa_k_sample = jnp.stack([st[3] for st in states])
    swa_v_sample = jnp.stack([st[4] for st in states])
    gla_state_sample = jnp.stack([st[5] for st in states])
    return (y_p, y_s, swa_k_prompt, swa_v_prompt, gla_state_prompt, swa_k_sample, swa_v_sample, gla_state_sample)


_drawn_inputs = setup_inputs


def setup_inputs(seed=0):
    import zlib

    import numpy as np

    out = dict(_drawn_inputs(seed))
    spreads = {}
    factors = {'q_norm': 7.651,
     'k_norm': 5.986,
     'sinks': 35.031,
     'b_gk': 13.007,
     'b1': 8.0,
     'b2': 8.0,
     'gla_norm': 2.897}
    for name, (base, spread) in spreads.items():
        noise = np.random.default_rng([zlib.crc32(name.encode()), seed]).standard_normal(out[name].shape)
        drawn = base * np.exp(spread * noise) if base else spread * noise
        out[name] = __import__('jax').numpy.asarray(drawn.astype(out[name].dtype))
    for name, factor in factors.items():
        out[name] = (out[name] * factor).astype(out[name].dtype)
    return out
```

```python
from contextlib import ExitStack

import numpy as np

import concourse.bass as bass
from concourse import mybir

F32 = mybir.dt.float32
I32 = mybir.dt.int32
U32 = mybir.dt.uint32
ALU = mybir.AluOpType
ACT = mybir.ActivationFunctionType
AX = mybir.AxisListType

P = 128
D = 1024
KD = D // P
PROMPT, NSEQ, TSEQ = 256, 8, 8
T = PROMPT + NSEQ * TSEQ
TILES = [(0, 128), (128, 128), (256, 64)]
HEADS, KVH, HD = 8, 2, 64
GROUP = HEADS // KVH
GH, GDK, GDV, RANK = 4, 64, 128, 16
PAIRS = GH // 2
CHUNK = 32
NCH = PROMPT // CHUNK
CPT = P // CHUNK
EXPERTS, TOPK, FF = 32, 4, 1024
SLOTS = 64
PASSES = T // SLOTS
KF = FF // P
NORM_EPS, QK_EPS, NEG = 1e-5, 1e-6, -1e30
SCALE = 0.125
GATE_NORM = 16.0

C_Q, C_K, C_V, C_QB, C_KB, C_VB = 0, 512, 640, 768, 1024, 1280
C_GLOW, C_RB, C_GA, C_GB = 1792, 1808, 2320, 3344
UNIT = 256
W_UNITS = [C_K, C_QB, C_KB, C_VB, C_VB + UNIT] + [C_RB + UNIT * i for i in range(2)] \
    + [C_GA + UNIT * i for i in range(4)] + [C_GB + UNIT * i for i in range(4)]
NU = 2 + len(W_UNITS)
RING = 12
FIRST_SLOT, STREAM_SLOTS = 6, 6

TILE_ORDER = [("q", j) for j in range(4)] + [("k", 0)] + [("va", t) for t in range(3)] \
    + [("qb", j) for j in range(2)] + [("kb", j) for j in range(2)] + [("glow", 0)] \
    + [("vb", t) for t in range(3)] + [("rb", j) for j in range(4)] \
    + [("ga", j) for j in range(8)] + [("gb", j) for j in range(8)]
FIRST_RB = 16

N_USES = ["rows", "b1"] + [f"norm{j}" for j in range(5)] + ["keys"] + [f"attend{s}" for s in range(5)] \
    + [f"gkeys{t}" for t in range(3)] + [f"dv{h}" for h in range(GH)]
XY_USES = ["z"] + [f"scores{s}" for s in range(5)] + ["decays_p", "decays_s"] + [f"state{w}" for w in range(4)]
VW_USES = ["cache"] + [f"probs{s}" for s in range(5)] + ["gla_p", "gla_s"]


def use(uses, name):
    return uses.index(name) + 1


def tiles_done(kind, j):
    return TILE_ORDER.index((kind, j)) + 1


def unit_done(m):
    last = [("q", 1), ("q", 3), ("va", 2), ("qb", 1), ("kb", 1), ("vb", 2), ("vb", 2)]
    return tiles_done(*last[m]) if m < len(last) else FIRST_RB + 2 * (m - 6)


CONST_AT, _at = {}, 0
for _name, _w in [("ident", 128), ("head_mean", 128), ("dv_mean", 128), ("before", 128), ("ones", 128),
                  ("band", 256), ("sample_mask", 384), ("gla_mask", 128), ("gla_smask", 64),
                  ("chunk_of", 4), ("seq_of", 8), ("head_of", 4), ("keep", 320), ("slot", 128),
                  ("expert", 32)]:
    CONST_AT[_name] = (_at, _w)
    _at += _w
NCONST = _at


def constants():
    c = {n: np.zeros((P, w), np.float32) for n, (_, w) in CONST_AT.items()}
    p = np.arange(P)
    c["ident"][:] = np.eye(P)
    c["head_mean"][:] = (p[:, None] // HD == p[None] // HD) / HD
    c["dv_mean"][:] = 1.0 / GDV
    c["before"][:] = p[:, None] < p[None]
    c["ones"][:] = 1.0
    key = np.arange(2 * P)[None]
    c["band"][:] = np.where((key > p[:, None]) & (key <= p[:, None] + P), 0.0, NEG)
    seq, tok = p // 32, p % 8
    for half in range(2):
        key = np.arange(P)[None]
        old = key > tok[:, None]
        new = np.arange(NSEQ * TSEQ)[None]
        new = (new // TSEQ == (4 * half + seq)[:, None]) & (new % TSEQ <= tok[:, None])
        c["sample_mask"][:, 192 * half:192 * half + 192] = np.where(np.concatenate([old, new], 1), 0.0, NEG)
    c["gla_mask"][:] = (p[:, None] // CHUNK == p[None] // CHUNK) & (p[:, None] <= p[None])
    s = np.arange(64)
    c["gla_smask"][:64] = (s[:, None] // TSEQ == s[None] // TSEQ) & (s[:, None] <= s[None])
    c["chunk_of"][:] = p[:, None] // CHUNK == np.arange(4)[None]
    c["seq_of"][:] = p[:, None] // TSEQ == np.arange(8)[None]
    c["head_of"][:] = p[:, None] % 32 // 8 == np.arange(4)[None]
    t = np.arange(T)
    c["keep"][:] = np.where(t < PROMPT, t % CHUNK != 0, t % TSEQ != 0)
    c["slot"][:] = np.arange(P) % SLOTS
    c["expert"][:] = np.arange(EXPERTS)
    return np.concatenate([c[n] for n in CONST_AT], 1)


def layer(nc: bass.Bass, x_prompt, x_sample, cache_k, cache_v, state_gla, norm1, w_in, q_norm, k_norm,
          sinks, w_gk, b_gk, gla_norm, w_a, w_b, w_o, norm2, w_router, b_router, w1, b1, w2, b2, consts,
          y_prompt, y_sample, k_prompt, v_prompt, s_prompt, k_sample, v_sample, s_sample):
    with ExitStack() as ctx:
        def sb(name, shape, dt=F32):
            return ctx.enter_context(nc.sbuf_tensor(name, shape, dt))

        def sem(name):
            return ctx.enter_context(nc.semaphore(name))

        ring = sb("ring", [P, RING, 2048])
        cst = sb("cst", [P, NCONST])
        acc = sb("acc", [P, 3, D])
        region2 = sb("region2", [P, 3 * D])
        xnT = sb("xnT", [P, KD, T])
        region_q = sb("region_q", [P, 2304])
        kT = sb("kT", [P, T])
        qbT = sb("qbT", [P, PAIRS, T])
        kbT = sb("kbT", [P, PAIRS, T])
        vA = sb("vA", [P, 3, P])
        vB = sb("vB", [P, 3, GH * GDV])
        rbT = sb("rbT", [P, GH, T])
        rsT = sb("rsT", [P, GH, T])
        gaT = sb("gaT", [P, KD, T])
        gbT = sb("gbT", [P, KD, T])
        oT = sb("oT", [P, GROUP, T])
        b1T = sb("b1T", [P, EXPERTS, 2, KF])
        b2r = sb("b2r", [EXPERTS, D])
        w_glow = sb("w_glow", [P, KD, RANK])
        w_rt = sb("w_rt", [P, KD, EXPERTS])
        b_rt = sb("b_rt", [P, EXPERTS])
        wgk = sb("wgk", [RANK, GH * GDK])
        sinkc = sb("sinkc", [P, HEADS])
        sink_s = sb("sink_s", [P, KVH, GROUP])
        sinkr = sb("sinkr", [P, 3, 4])
        rows = sb("rows", [21, P])
        cols = sb("cols", [P, 21])
        kTok = sb("kTok", [P, 2, P])
        small = sb("small", [P, 64])
        dec = sb("dec", [P, PAIRS, NCH + NSEQ])
        sel = sb("sel", [P, 3, EXPERTS])
        gates = sb("gates", [P, 3, EXPERTS + 2])
        place = sb("place", [P, 3, EXPERTS + 2])
        most = sb("most", [1, 1], I32)

        def const(name, rows_=P):
            a, w = CONST_AT[name]
            return cst[0:rows_, a:a + w]

        ident = const("ident")
        late = ring[:, 4:6, :].rearrange("p a b -> p (a b)")
        ck = late[:, 0:1024].rearrange("p (b c) -> p b c", b=NSEQ)
        cv = late[:, 1024:2048].rearrange("p (b c) -> p b c", b=NSEQ)
        ckT = late[:, 2048:3072].rearrange("p (b c) -> p b c", b=NSEQ)
        S_at = late[:, 3072:4096]
        low = ring[:, 0:4, :].rearrange("p a b -> p (a b)")
        PT_ = PAIRS * T
        zb, lsp, B, D1, D2, q_in, k_in, q_out, k_out = (
            low[:, i * PT_:(i + 1) * PT_].rearrange("p (j t) -> p j t", j=PAIRS) for i in range(9))
        S_all = low[:, 9 * PT_:9 * PT_ + (NCH + 1) * 256].rearrange("p (c j v) -> p c j v", j=PAIRS, v=GDV)
        glT = low[0:RANK, 3 * PT_:3 * PT_ + T]
        AT_p = low[:, 0:1024].rearrange("p (h t j s) -> p h t j s", h=2, t=2, j=PAIRS)
        AT_s = low[:, 1024:1280].rearrange("p (h j s) -> p h j s", h=2, j=PAIRS)
        xn = region2[:, :].rearrange("p (t c) -> p t c", t=3)
        kM = region2[:, 0:1024].rearrange("p (c k) -> p c k", c=CPT)
        kMs = region2[:, 1024:3072].rearrange("p (c k) -> p c k", c=NSEQ)
        obT = region2[:, 1024:1024 + GH * T].rearrange("p (h t) -> p h t", h=GH)
        scratch = acc[:, :, :].rearrange("p t c -> p (t c)")
        raw = scratch[:, 0:640].rearrange("p (b t) -> p b t", b=2)
        squares = scratch[:, 640:1280].rearrange("p (b t) -> p b t", b=2)
        rstd_qk = scratch[:, 1280:1920].rearrange("p (b t) -> p b t", b=2)
        S0 = scratch[:, 0:2048].rearrange("p (b j v) -> p b j v", b=NSEQ, j=PAIRS)
        b1r = gbT[0:EXPERTS, :, :].rearrange("p a b -> p (a b)")[:, 0:2 * FF]
        qT = region_q[:, 0:1024].rearrange("p (j t) -> p j t", j=4)
        qS = region_q[:, 1024:1280].rearrange("p (b j t) -> p b j t", b=NSEQ, j=4)
        pT = region_q[:, 1280:2304].rearrange("p (k h q) -> p k h q", k=2, h=4)
        S_new = region_q[:, 0:2048].rearrange("p (b j v) -> p b j v", b=NSEQ, j=PAIRS)
        squares_o = xnT[:, 0:4, :]
        rstd_o = xnT[:, 4:8, :]
        hnT = gaT
        moe = gbT[:, :, :].rearrange("p a b -> p (a b)")
        hn = region2[:, :].rearrange("p (t c) -> p t c", t=3)
        xeT = moe[:, 0:1024].rearrange("p (k s) -> p k s", k=KD)
        u_sb = moe[:, 1024:2048].rearrange("p (q c) -> p q c", q=2)
        moe2 = xnT[:, :, :].rearrange("p a b -> p (a b)")
        y_sb = moe2[:, 0:1024].rearrange("p (s c) -> p s c", s=2)
        hT = moe2[:, 1024:2048].rearrange("p (s f t) -> p s f t", s=2, f=KF)
        glu = moe2[:, 2048:2560].rearrange("p (f t) -> p f t", f=KF)
        moe3 = rbT[:, :, :].rearrange("p a b -> p (a b)")
        lin = moe3[:, 0:512].rearrange("p (f t) -> p f t", f=KF)
        sig = moe3[:, 512:1024].rearrange("p (f t) -> p f t", f=KF)
        pick = rsT[:, :, :].rearrange("p a b -> p (a b)")[:, 0:384].rearrange("p (t s) -> p t s", t=3)
        moe4 = oT[:, :, :].rearrange("p a b -> p (a b)")
        gpick = moe4[:, 0:768].rearrange("p (t s c) -> p t s c", t=3, s=2)
        gateT = moe4[0:EXPERTS, 768:768 + T]
        gpickT = rsT[:, :, :].rearrange("p a b -> p (a b)")[:, 384:1152].rearrange("p (s t) -> p s t", s=2)
        rt = qbT[:, :, :].rearrange("p a b -> p (a b)")
        lg = rt[:, 0:32]
        top8 = rt[:, 32:40]
        idxf = rt[:, 48:52]
        top_e = rt[:, 52:56]
        onehot = rt[:, 64:192].rearrange("p (k e) -> p k e", k=TOPK)
        onehot_g = rt[:, 192:320].rearrange("p (k e) -> p k e", k=TOPK)
        idx8 = sb("idx8", [P, 8], U32)

        ps = ctx.enter_context(nc.psum_tensor("ps", [P, 8, 512], F32))
        NB, XB, YB, VB_, WB = 3, 4, 5, 6, 7

        ident_in, consts_in, rows_in, x_in, small_in, cache_in = (sem(n) for n in (
            "ident_in", "consts_in", "rows_in", "x_in", "small_in", "cache_in"))
        b1_in = sem("b1_in")
        unit_in = [sem(f"unit_in{m}") for m in range(NU)]
        wa_in, wb_in, wo_in, s0_in, x_again = (sem(n) for n in ("wa_in", "wb_in", "wo_in", "s0_in", "x_again"))
        ss_ready, rstd_base, rstd_ready, xn_ready = (sem(n) for n in ("ss_ready", "rstd_base", "rstd_ready", "xn_ready"))
        xT_ready, xnT_ready = sem("xT_ready"), sem("xnT_ready")
        pj_ready, pj_freed = sem("pj_ready"), sem("pj_freed")
        sq_ready, var_ready, qk_rstd, qk_done = (sem(n) for n in ("sq_ready", "var_ready", "qk_rstd", "qk_done"))
        n_ready, n_freed = sem("n_ready"), sem("n_freed")
        xy_ready, xy_freed = sem("xy_ready"), sem("xy_freed")
        vw_ready, vw_freed = sem("vw_ready"), sem("vw_freed")
        lsp_ready, decay_ready, exps_ready, gla_ops = (sem(n) for n in ("lsp_ready", "decay_ready", "exps_ready", "gla_ops"))
        max_ready, exp_done, p_ready = sem("max_ready"), sem("exp_done"), sem("p_ready")
        pads_ready, sqo_ready, varo_ready, rstdo_ready, ob_done = (sem(n) for n in (
            "pads_ready", "sqo_ready", "varo_ready", "rstdo_ready", "ob_done"))
        merged_ready, mg_ready, mg_freed = (sem(n) for n in ("merged_ready", "mg_ready", "mg_freed"))
        h_psum, h_ready, ss2_ready, base2_ready, rstd2_ready, hn_ready, hnT_psum, hnT_ready, lg_psum = (sem(n) for n in (
            "h_psum", "h_ready", "ss2_ready", "base2_ready", "rstd2_ready", "hn_ready", "hnT_psum", "hnT_ready", "lg_psum"))
        top_ready, gexp_ready, route_ready, pos_psum, gT_copied, place_ready = (sem(n) for n in (
            "top_ready", "gexp_ready", "route_ready", "pos_psum", "gT_copied", "place_ready"))
        lgt_freed = sem("lgt_freed")
        act_steps, dve_steps = sem("act_steps"), sem("dve_steps")
        states_out, y_out = sem("states_out"), sem("y_out")
        stores, count_ready, slots_moved = sem("stores"), sem("count_ready"), sem("slots_moved")
        w1_in = [sem(f"w1_in{k}") for k in range(KD)]
        w2_in = [sem(f"w2_in{j}") for j in range(4)]
        w1_used, w2_used = sem("w1_used"), sem("w2_used")
        pick_ready, gpick_ready, gather_done, xe_ready, gpT_done, gpT_copied = (sem(n) for n in (
            "pick_ready", "gpick_ready", "gather_done", "xe_ready", "gpT_done", "gpT_copied"))
        u_copied, ut_done, glu_biased, glu_ready, lin_biased, lin_ready, sig_ready, prod_ready, h_act = (sem(n) for n in (
            "u_copied", "ut_done", "glu_biased", "glu_ready", "lin_biased", "lin_ready", "sig_ready", "prod_ready", "h_act"))
        y_copied, comb_done, comb_added, acc_final = (sem(n) for n in ("y_copied", "comb_done", "comb_added", "acc_final"))

        def slot_of(m):
            return FIRST_SLOT + m % STREAM_SLOTS

        def unit(m):
            return ring[:, slot_of(m), :].rearrange("p (k c) -> p k c", k=KD)

        wa_sb = ring[:, 6:8, :].rearrange("p a b -> p (a b)").rearrange("p (k c) -> p k c", k=4)
        wb_sb = ring[:, 4:6, :].rearrange("p a b -> p (a b)").rearrange("p (k c) -> p k c", k=4)
        wo_sb = ring[:, 8:12, :].rearrange("p a b -> p (a b)").rearrange("p (k c) -> p k c", k=KD)
        w1v = w1.rearrange("l e (k p) c -> (l e) k p c", p=P)
        w2v = w2.rearrange("l e (j f p) c -> (l e) j p f c", f=2, p=P)

        def x_tile(t):
            return x_sample.rearrange("b t c -> (b t) c") if t == 2 else x_prompt[0, t * P:(t + 1) * P, :]

        def order_of(f):
            return f // 4 * 4 + f % 2 * 2 + f // 2 % 2

        block = ctx.enter_context(nc.Block())

        @block.sync
        def _(sp):
            sp.dma_start(cst[:, 0:P], consts[:, 0:P]).then_inc(ident_in, 16)
            for t, (_, r) in enumerate(TILES):
                sp.dma_start(acc[0:r, t, :], x_tile(t)).then_inc(x_in, 16)
            for m in range(2):
                for j in range(2):
                    for g in range(KVH):
                        h = GROUP * g + 2 * m + j
                        sp.dma_start(unit(m)[:, :, P * j + HD * g:P * j + HD * g + HD],
                                     w_in[0, :, h * HD:(h + 1) * HD].rearrange("(k p) c -> p k c", p=P)
                                     ).then_inc(unit_in[m], 16)
                if m == 0:
                    sp.dma_start(cst[:, P:NCONST], consts[:, P:NCONST]).then_inc(consts_in, 16)

            def load_unit(m):
                c = W_UNITS[m - 2]
                sp.dma_start(unit(m), w_in[0, :, c:c + UNIT].rearrange("(k p) c -> p k c", p=P)
                             ).then_inc(unit_in[m], 16)

            for m in range(2, STREAM_SLOTS):
                load_unit(m)
            for m in range(STREAM_SLOTS, NU):
                sp.wait_ge(pj_ready, unit_done(m - STREAM_SLOTS))
                load_unit(m)
                if m == STREAM_SLOTS + 2:
                    sp.wait_ge(qk_done, 5)
                    sp.dma_start(S0.rearrange("p b j v -> p (b j) v"),
                                 state_gla[0].rearrange("b (j a) k v -> (a k) (b j) v", a=2)).then_inc(s0_in, 16)
            sp.wait_ge(pj_ready, unit_done(13))
            for g in range(KVH):
                sp.dma_start(wa_sb[HD * g:HD * g + HD, :, :],
                             w_a[0, 256 * g:256 * g + 256, :].rearrange("(j d) c -> d j c", d=HD)).then_inc(wa_in, 16)
            sp.wait_ge(n_ready, use(N_USES, "attend4"))
            sp.dma_start(wb_sb, w_b[0].rearrange("(h v) c -> v h c", v=GDV)).then_inc(wb_in, 16)
            sp.wait_ge(pj_ready, len(TILE_ORDER))
            sp.dma_start(wo_sb, w_o[0].rearrange("(k p) c -> p k c", p=P)).then_inc(wo_in, 16)
            sp.wait_ge(vw_ready, use(VW_USES, "gla_s"))
            sp.wait_ge(xy_freed, use(XY_USES, "state3"))
            for t, (_, r) in enumerate(TILES):
                sp.dma_start(acc[0:r, t, :], x_tile(t)).then_inc(x_again, 16)

            def load_w1(n, e, k):
                sp.dma_start(ring[:, k, :], w1v[e, k]).then_inc(w1_in[k], 16)

            def load_w2(n, e, j):
                sp.dma_start(ring[:, 8 + j, :].rearrange("p (f c) -> p f c", f=2), w2v[e, j]).then_inc(w2_in[j], 16)

            def next_w1(n, e):
                for k in range(KD):
                    sp.wait_ge(w1_used, (n - 1) * KD + k + 1)
                    load_w1(n, e, k)

            def next_w2(n, e):
                for j in range(4):
                    sp.wait_ge(w2_used, (n - 1) * 4 + j + 1)
                    load_w2(n, e, j)

            sp.wait_ge(states_out, 16)
            for k in range(4):
                load_w1(0, 0, k)
            sp.wait_ge(merged_ready, KD)
            for k in range(4, KD):
                load_w1(0, 0, k)
            sp.wait_ge(h_psum, 3)
            for j in range(4):
                load_w2(0, 0, j)
            next_w1(1, 1)
            with sp.Fori(1, EXPERTS // 2) as i:
                next_w2(2 * i - 1, 2 * i - 1)
                next_w1(2 * i, 2 * i)
                next_w1(2 * i + 1, 2 * i + 1)
                next_w2(2 * i, 2 * i)
            next_w2(EXPERTS - 1, EXPERTS - 1)
            sp.wait_ge(count_ready, 1)
            busiest = sp.value_load(most[0:1, 0:1], min_val=0, max_val=T)
            with sp.If(busiest > SLOTS):
                with sp.Fori(1, PASSES) as b:
                    next_w1(EXPERTS * b, 0)
                    next_w1(EXPERTS * b + 1, 1)
                    next_w2(EXPERTS * b, 0)
                    with sp.Fori(1, EXPERTS // 2) as i:
                        next_w2(EXPERTS * b + 2 * i - 1, 2 * i - 1)
                        next_w1(EXPERTS * b + 2 * i, 2 * i)
                        next_w1(EXPERTS * b + 2 * i + 1, 2 * i + 1)
                        next_w2(EXPERTS * b + 2 * i, 2 * i)
                    next_w2(EXPERTS * b + EXPERTS - 1, EXPERTS - 1)
                sp.nop()
            sp.nop()
            sp.wait_ge(acc_final, 1)
            for t, (_, r) in enumerate(TILES):
                dst = y_sample.rearrange("b t c -> (b t) c") if t == 2 else y_prompt[0, t * P:(t + 1) * P, :]
                sp.dma_start(dst, acc[0:r, t, :]).then_inc(y_out, 16)
            sp.wait_ge(stores, 16 * 21)
            sp.wait_ge(y_out, 16 * 3)

        @block.gpsimd
        def _(pool):
            pool.dma_start(rows[0:8, :], norm1.rearrange("l (k p) -> (l k) p", p=P)).then_inc(rows_in, 16)
            pool.dma_start(rows[8:16, :], norm2.rearrange("l (k p) -> (l k) p", p=P)).then_inc(rows_in, 16)
            pool.dma_start(rows[16:18, :], b_gk.rearrange("l (k p) -> (l k) p", p=P)).then_inc(rows_in, 16)
            for g in range(KVH):
                pool.dma_start(rows[18:19, HD * g:HD * g + HD], q_norm).then_inc(rows_in, 16)
                pool.dma_start(rows[19:20, HD * g:HD * g + HD], k_norm).then_inc(rows_in, 16)
            pool.dma_start(rows[20:21, :], gla_norm).then_inc(rows_in, 16)
            pool.dma_start(b1r, b1[0]).then_inc(b1_in, 16)
            pool.dma_start(w_glow[:, :, :], w_in[0, :, C_GLOW:C_RB].rearrange("(k p) c -> p k c", p=P)).then_inc(small_in, 16)
            pool.dma_start(wgk[:, :], w_gk[0]).then_inc(small_in, 16)
            pool.dma_start(sinkc[:, :], sinks.partition_broadcast(P).rearrange("p a h -> p (a h)")).then_inc(small_in, 16)
            pool.dma_start(ck, cache_k[0].rearrange("b w g d -> w b (g d)")).then_inc(cache_in, 16)
            pool.dma_start(cv, cache_v[0].rearrange("b w g d -> w b (g d)")).then_inc(cache_in, 16)
            pool.dma_start(w_rt[:, :, :], w_router[0].rearrange("(k p) e -> p k e", p=P)).then_inc(small_in, 16)
            pool.dma_start(b_rt[:, :], b_router.partition_broadcast(P).rearrange("p a h -> p (a h)")).then_inc(small_in, 16)
            pool.dma_start(b2r[:, :], b2[0]).then_inc(small_in, 16)
            pool.memset(place[:, :, :], -1.0).then_inc(pads_ready, 1)
            pool.memset(gates[:, :, :], 0.0).then_inc(pads_ready, 1)
            pool.memset(sel[:, :, :], 0.0).then_inc(pads_ready, 1)
            pool.wait_ge(pads_ready, 3)
            pool.memset(vB[64:128, 2, :], 0.0).then_inc(pads_ready, 1)
            for dst, src in ((k_sample, cache_k), (v_sample, cache_v)):
                pool.dma_start(dst[0, :, 0:P - TSEQ].rearrange("b w g d -> b w (g d)"),
                               src[0, :, TSEQ:P].rearrange("b w g d -> b w (g d)")).then_inc(stores, 16)
            pool.wait_ge(pj_freed, 8)
            pool.dma_start(v_prompt[0, 0].rearrange("w g d -> w (g d)"), vA[:, 1, :]).then_inc(stores, 16)
            for b in range(NSEQ):
                pool.dma_start(v_sample[0, b, P - TSEQ:P].rearrange("w g d -> w (g d)"),
                               vA[TSEQ * b:TSEQ * b + TSEQ, 2, :]).then_inc(stores, 16)
            pool.wait_ge(n_freed, use(N_USES, "keys"))
            pool.dma_start(k_prompt[0, 0].rearrange("w g d -> w (g d)"), kTok[:, 0, :]).then_inc(stores, 16)
            for b in range(NSEQ):
                pool.dma_start(k_sample[0, b, P - TSEQ:P].rearrange("w g d -> w (g d)"),
                               kTok[TSEQ * b:TSEQ * b + TSEQ, 1, :]).then_inc(stores, 16)
            pool.wait_ge(xy_freed, use(XY_USES, "state3"))
            pool.dma_start(s_prompt[0, 0].rearrange("(j a) k v -> (a k) j v", a=2), S_all[:, NCH, :, :]).then_inc(states_out, 16)
            pool.dma_start(s_sample[0].rearrange("b (j a) k v -> (a k) (b j) v", a=2),
                           S_new.rearrange("p b j v -> p (b j) v")).then_inc(stores, 16)

        @block.tensor
        def _(pe):
            def take(uses, freed, name):
                if use(uses, name) > 1:
                    pe.wait_ge(freed, use(uses, name) - 1)

            pe.wait_ge(ident_in, 16)
            pe.wait_ge(rows_in, 16 * 8)
            pe.transpose(ps[:, NB, 0:21], rows[:, :], ident[0:21, 0:21]).then_inc(n_ready, 1)
            for t, (_, r) in enumerate(TILES):
                pe.wait_ge(xn_ready, t + 1)
                for half in range(2):
                    u = 2 * t + half
                    if u >= 4:
                        pe.wait_ge(xnT_ready, u - 3)
                    for k in range(4):
                        mm = pe.transpose(ps[:, XB + u % 4, P * k:P * k + r],
                                          xn[0:r, t, P * (4 * half + k):P * (4 * half + k) + P], ident[0:r, 0:r])
                    mm.then_inc(xT_ready, 1)

            pe.wait_ge(xnT_ready, 6)
            pe.wait_ge(consts_in, 16)

            def b1_to_columns():
                pe.wait_ge(b1_in, 16)
                take(N_USES, n_freed, "b1")
                for gl in range(2):
                    for f in range(KF):
                        c = 256 * f + gl
                        mm = pe.transpose(ps[:, NB, (gl * KF + order_of(f)) * EXPERTS:(gl * KF + order_of(f) + 1) * EXPERTS],
                                          b1r[:, c:c + 255:2], ident[0:EXPERTS, 0:EXPERTS])
                mm.then_inc(n_ready, 1)

            unit_at = [0]

            def need_unit(m):
                if m >= unit_at[0]:
                    pe.wait_ge(unit_in[m], 64 if m < 2 else 16)
                    unit_at[0] = m + 1

            def project(n):
                kind, j = TILE_ORDER[n]
                bank = n % 3
                if n >= 3:
                    pe.wait_ge(pj_freed, n - 2)
                if kind in ("va", "vb"):
                    t0, r = TILES[j]
                    if kind == "va":
                        for k in range(KD):
                            mm = pe.matmul(ps[0:r, bank, 0:P], xnT[:, k, t0:t0 + r], unit(2)[:, k, P:2 * P],
                                           start=(k == 0), stop=(k == KD - 1))
                    else:
                        for c in range(2):
                            need_unit(5 + c)
                        for c in range(2):
                            for k in range(KD):
                                mm = pe.matmul(ps[0:r, bank, UNIT * c:UNIT * c + UNIT], xnT[:, k, t0:t0 + r],
                                               unit(5 + c)[:, k, :], start=(k == 0), stop=(k == KD - 1))
                    mm.then_inc(pj_ready, 1)
                    return
                if kind == "glow":
                    pe.wait_ge(small_in, 16 * 6)
                    for k in range(KD):
                        mm = pe.matmul(ps[0:RANK, bank, 0:T], w_glow[:, k, :], xnT[:, k, :],
                                       start=(k == 0), stop=(k == KD - 1))
                    mm.then_inc(pj_ready, 1)
                    return
                m = {"q": 0, "k": 2, "qb": 3, "kb": 4, "rb": 7, "ga": 9, "gb": 13}[kind] + j // 2
                need_unit(m)
                c = P * (j % 2)
                for k in range(KD):
                    mm = pe.matmul(ps[:, bank, 0:T], unit(m)[:, k, c:c + P], xnT[:, k, :],
                                   start=(k == 0), stop=(k == KD - 1))
                mm.then_inc(pj_ready, 1)

            def norm_sum(j):
                take(N_USES, n_freed, f"norm{j}")
                pe.wait_ge(sq_ready, j + 1)
                pe.matmul(ps[:, NB, 0:T], const("head_mean"), squares[:, j % 2, :], start=True, stop=True
                          ).then_inc(n_ready, 1)

            def gate_logits():
                take(XY_USES, xy_freed, "z")
                pe.wait_ge(pj_freed, tiles_done("glow", 0))
                for j in range(PAIRS):
                    mm = pe.matmul(ps[:, XB + j, 0:T], wgk[:, P * j:P * j + P], glT[:, :], start=True, stop=True)
                mm.then_inc(xy_ready, 1)

            def cache_keys():
                take(VW_USES, vw_freed, "cache")
                pe.wait_ge(cache_in, 32)
                for b in range(NSEQ):
                    mm = pe.transpose(ps[:, VB_ + b // 4, P * (b % 4):P * (b % 4) + P], ck[:, b, :], ident)
                mm.then_inc(vw_ready, 1)

            def new_keys():
                take(N_USES, n_freed, "keys")
                pe.wait_ge(qk_done, 5)
                pe.transpose(ps[:, NB, 0:P], kT[:, P:2 * P], ident)
                pe.transpose(ps[0:64, NB, P:2 * P], kT[:, PROMPT:T], ident).then_inc(n_ready, 1)

            def scores(s):
                take(XY_USES, xy_freed, f"scores{s}")
                if s < 4:
                    n, i = divmod(s, 2)
                    first = 0 if n else P
                    w = 256 if n else P
                    for jj in range(2):
                        for g in range(KVH):
                            mm = pe.matmul(ps[:, XB + g, 256 * jj:256 * jj + w],
                                           qT[HD * g:HD * g + HD, 2 * i + jj, P * n:P * n + P],
                                           kT[HD * g:HD * g + HD, P * n - P + first:P * n + P], start=True, stop=True)
                else:
                    pe.wait_ge(vw_freed, 1)
                    for b in range(NSEQ):
                        hf, q = divmod(b, 4)
                        for g in range(KVH):
                            lhs = qS[HD * g:HD * g + HD, b, :, :].rearrange("p j t -> p (j t)")
                            out = ps[32 * q:32 * q + 32, XB + g, 192 * hf:192 * hf + 192]
                            pe.matmul(out[:, 0:P], lhs, ckT[HD * g:HD * g + HD, b, :], start=True, stop=True)
                            mm = pe.matmul(out[:, P:192], lhs, kT[HD * g:HD * g + HD, PROMPT:T], start=True, stop=True)
                mm.then_inc(xy_ready, 1)

            S_p = [S_at.rearrange("p (h c) -> p h c", h=4), S_at[:, 0:768].rearrange("p (h c) -> p h c", h=4)]

            def turn_probs(s):
                take(VW_USES, vw_freed, f"probs{s}")
                pe.wait_ge(p_ready, s + 1)
                for h in range(4):
                    if s < 4:
                        if s >= 2:
                            pe.transpose(ps[:, VB_, P * h:P * h + P], S_p[0][:, h, 0:P], ident)
                        mm = pe.transpose(ps[:, WB, P * h:P * h + P], S_p[0][:, h, P:2 * P], ident)
                    else:
                        pe.transpose(ps[:, VB_, P * h:P * h + P], S_p[1][:, h, 0:P], ident)
                        mm = pe.transpose(ps[0:64, WB, P * h:P * h + P], S_p[1][:, h, P:192], ident)
                mm.then_inc(vw_ready, 1)

            def attend(s):
                take(N_USES, n_freed, f"attend{s}")
                pe.wait_ge(vw_freed, use(VW_USES, f"probs{s}"))
                for g in range(KVH):
                    out = ps[HD * g:HD * g + HD, NB, :]
                    if s < 4:
                        blocks = [1] if s < 2 else [0, 1]
                        for kb in blocks:
                            mm = pe.matmul(out[:, 0:256], vA[:, s // 2 - 1 + kb, HD * g:HD * g + HD],
                                           pT[:, kb, 2 * g:2 * g + 2, :].rearrange("p h q -> p (h q)"),
                                           start=(kb == blocks[0]), stop=(kb == 1))
                    else:
                        for hf in range(2):
                            pe.matmul(out[:, P * hf:P * hf + P], vA[0:64, 2, HD * g:HD * g + HD], pT[0:64, 1, 2 * g + hf, :],
                                      start=True, stop=False, skip_group_check=True)
                            for q in range(4):
                                mm = pe.matmul(out[:, P * hf + 32 * q:P * hf + 32 * q + 32],
                                               cv[:, 4 * hf + q, HD * g:HD * g + HD],
                                               pT[:, 0, 2 * g + hf, 32 * q:32 * q + 32],
                                               start=False, stop=(q == 3), skip_group_check=True)
                mm.then_inc(n_ready, 1)

            def decays(name, tiles):
                take(XY_USES, xy_freed, name)
                pe.wait_ge(gla_ops, 1)
                for t in tiles:
                    t0, r = TILES[t]
                    for j in range(PAIRS):
                        for a in range(2):
                            at = P * (2 * t + j) if t < 2 else 64 * j
                            mm = pe.matmul(ps[0:r, XB + a, at:at + r], k_in[64 * a:64 * a + 64, j, t0:t0 + r],
                                           q_in[64 * a:64 * a + 64, j, t0:t0 + r], start=True, stop=True)
                mm.then_inc(xy_ready, 1)

            def turn_keys(t):
                take(N_USES, n_freed, f"gkeys{t}")
                pe.wait_ge(gla_ops, 1)
                t0, r = TILES[t]
                for j in range(PAIRS):
                    mm = pe.transpose(ps[0:r, NB, P * j:P * j + P], k_out[:, j, t0:t0 + r], ident)
                mm.then_inc(n_ready, 1)

            def state_steps(which):
                take(XY_USES, xy_freed, f"state{which}")
                pe.wait_ge(n_freed, use(N_USES, f"gkeys{min(which, 2)}"))
                t = min(which, 2)
                r = TILES[t][1]
                for c in range(4):
                    keys = kM[:, c, :] if which < 2 else kMs[0:64, 4 * (which - 2) + c, :]
                    for j in range(PAIRS):
                        for a in range(2):
                            o = 256 * (c % 2) + P * j
                            mm = pe.matmul(ps[64 * a:64 * a + 64, XB + c // 2, o:o + P],
                                           keys[:, P * j + 64 * a:P * j + 64 * a + 64],
                                           vB[0:r, t, P * (2 * j + a):P * (2 * j + a) + P], start=True, stop=True)
                mm.then_inc(xy_ready, 1)

            def gla_out(sample):
                take(VW_USES, vw_freed, "gla_s" if sample else "gla_p")
                pe.wait_ge(xy_freed, use(XY_USES, "state1"))
                if sample:
                    pe.wait_ge(pads_ready, 4)
                    pe.wait_ge(s0_in, 16)
                for a in range(2):
                    for t in ([2] if sample else [0, 1]):
                        for j in range(PAIRS):
                            h = 2 * j + a
                            if sample:
                                out = ps[:, VB_ + a, 64 * j:64 * j + 64]
                                pe.matmul(out, vB[:, 2, P * h:P * h + P], AT_s[:, a, j, :], start=True, stop=False,
                                          skip_group_check=True)
                                for b in range(NSEQ):
                                    mm = pe.matmul(out[:, 8 * b:8 * b + 8], S0[64 * a:64 * a + 64, b, j, :],
                                                   q_out[64 * a:64 * a + 64, j, PROMPT + 8 * b:PROMPT + 8 * b + 8],
                                                   start=False, stop=(b == NSEQ - 1), skip_group_check=True)
                            else:
                                out = ps[:, VB_ + a, P * (2 * t + j):P * (2 * t + j) + P]
                                pe.matmul(out, vB[:, t, P * h:P * h + P], AT_p[:, a, t, j, :], start=True, stop=False,
                                          skip_group_check=True)
                                for c in range(CPT):
                                    if t == 0 and c == 0:
                                        continue
                                    s0 = t * P + CHUNK * c
                                    mm = pe.matmul(out[:, CHUNK * c:CHUNK * c + CHUNK],
                                                   S_all[64 * a:64 * a + 64, CPT * t + c, j, :],
                                                   q_out[64 * a:64 * a + 64, j, s0:s0 + CHUNK],
                                                   start=False, stop=(c == CPT - 1), skip_group_check=True)
                mm.then_inc(vw_ready, 1)

            def dv_sums():
                for h in range(GH):
                    take(N_USES, n_freed, f"dv{h}")
                    pe.wait_ge(sqo_ready, 1)
                    pe.matmul(ps[:, NB, 0:T], const("dv_mean"), squares_o[:, h, :], start=True, stop=True
                              ).then_inc(n_ready, 1)

            for n in range(FIRST_RB):
                project(n)
                if 1 <= n <= 5:
                    norm_sum(n - 1)
                if n == 0:
                    b1_to_columns()
            between = {
                0: [gate_logits, cache_keys],
                1: [new_keys, lambda: scores(0)],
                4: [lambda: turn_probs(0), lambda: scores(1)],
                5: [lambda: attend(0)],
                6: [lambda: turn_probs(1), lambda: scores(2)],
                7: [lambda: attend(1)],
                8: [lambda: turn_probs(2), lambda: scores(3)],
                9: [lambda: attend(2)],
                10: [lambda: turn_probs(3), lambda: scores(4)],
                11: [lambda: attend(3)],
                12: [lambda: turn_probs(4), lambda: decays("decays_p", [0, 1])],
                13: [lambda: attend(4), lambda: decays("decays_s", [2])],
                14: [lambda: turn_keys(0), lambda: state_steps(0)],
                15: [lambda: turn_keys(1), lambda: state_steps(1)],
                16: [lambda: turn_keys(2), lambda: state_steps(2)],
                17: [lambda: state_steps(3), lambda: gla_out(False)],
                18: [lambda: gla_out(True)],
            }
            for s in range(20):
                project(FIRST_RB + s)
                for step in between.get(s, ()):
                    step()

            def branch(w_sb, operand, m, u):
                if u < 3:
                    pe.wait_ge(pj_freed, len(TILE_ORDER))
                else:
                    pe.wait_ge(mg_freed, u - 2)
                for k in range(4):
                    mm = pe.matmul(ps[:, u % 3, 0:T], w_sb[:, k, P * m:P * m + P], operand[:, k, :],
                                   start=(k == 0), stop=(k == 3))
                mm.then_inc(mg_ready, 1)

            pe.wait_ge(wa_in, 32)
            pe.wait_ge(n_freed, use(N_USES, "attend4"))
            for m in range(KD):
                branch(wa_sb, oT, m, m)
                if m == 3:
                    dv_sums()
            pe.wait_ge(wb_in, 16)
            pe.wait_ge(ob_done, 1)
            for m in range(KD):
                branch(wb_sb, obT, m, KD + m)
            pe.wait_ge(wo_in, 16)
            pe.wait_ge(merged_ready, KD)
            for t, (t0, r) in enumerate(TILES):
                if t == 0:
                    pe.wait_ge(xy_freed, len(XY_USES))
                if t == 1:
                    pe.wait_ge(vw_freed, len(VW_USES))
                if t == 2:
                    pe.wait_ge(h_ready, 1)
                for c in range(2):
                    for k in range(KD):
                        mm = pe.matmul(ps[0:r, (XB, VB_, XB)[t] + c, :], xnT[:, k, t0:t0 + r],
                                       wo_sb[:, k, 512 * c:512 * c + 512], start=(k == 0), stop=(k == KD - 1))
                mm.then_inc(h_psum, 1)
            for t, (t0, r) in enumerate(TILES):
                pe.wait_ge(hn_ready, t + 1)
                if t:
                    pe.wait_ge(hnT_ready, t)
                else:
                    pe.wait_ge(mg_freed, 2 * KD)
                for k in range(KD):
                    mm = pe.transpose(ps[:, k // 4, P * (k % 4):P * (k % 4) + r], hn[0:r, t, P * k:P * k + P],
                                      ident[0:r, 0:r])
                mm.then_inc(hnT_psum, 1)
                pe.wait_ge(hnT_ready, t + 1)
                if t:
                    pe.wait_ge(lgt_freed, t)
                for k in range(KD):
                    mm = pe.matmul(ps[0:r, 2, 0:EXPERTS], hnT[:, k, t0:t0 + r], w_rt[:, k, :],
                                   start=(k == 0), stop=(k == KD - 1))
                mm.then_inc(lg_psum, 1)
            pe.wait_ge(route_ready, 3)
            pe.wait_ge(pads_ready, 4)
            pe.wait_ge(n_freed, len(N_USES))
            for t, (t0, r) in enumerate(TILES):
                for s in range(t + 1):
                    rr = TILES[s][1]
                    pe.matmul(ps[0:r, NB, EXPERTS * t:EXPERTS * (t + 1)],
                              (const("before") if s == t else const("ones"))[0:rr, 0:r], sel[0:rr, s, :],
                              start=(s == 0), stop=(s == t))
            for t, (_, r) in enumerate(TILES):
                mm = pe.matmul(ps[0:1, NB, 96:128], const("ones")[0:r, 0:1], sel[0:r, t, :],
                               start=(t == 0), stop=(t == 2))
            mm.then_inc(pos_psum, 1)
            pe.wait_ge(lgt_freed, 3)
            for t, (t0, r) in enumerate(TILES):
                mm = pe.transpose(ps[0:EXPERTS, 2, t0:t0 + r], gates[0:r, t, 0:EXPERTS], ident[0:r, 0:r])
            mm.then_inc(pos_psum, 1)

            def gather(p):
                for half in range(2):
                    if half == 0:
                        pe.wait_ge(pick_ready, p + 1)
                        pe.wait_ge(gpT_copied, 2 * p)
                    else:
                        pe.wait_ge(xe_ready, 2 * p + 1)
                    for k in range(4):
                        for t, (_, r) in enumerate(TILES):
                            c = P * (4 * half + k)
                            mm = pe.matmul(ps[:, 7, P * k:P * k + P], hn[0:r, t, c:c + P], pick[0:r, t, :],
                                           start=(t == 0), stop=(t == 2))
                    mm.then_inc(gather_done, 1)

            def up(n, which, first=False):
                if not first:
                    pe.wait_ge(u_copied, n)
                if which == 0:
                    pe.wait_ge(xe_ready, n + 2)
                for k in range(KD):
                    pe.wait_ge(w1_in[k], 16 * n + 16)
                    for q in range(4):
                        o = 64 * (q % 2)
                        mm = pe.matmul(ps[o:o + 64, q // 2, :], xeT[:, k, SLOTS * which:SLOTS * (which + 1)],
                                       ring[:, k, 512 * q:512 * q + 512], start=(k == 0), stop=(k == KD - 1))
                    mm.then_inc(w1_used, 1)

            def turn(n, first=False):
                pe.wait_ge(u_copied, n + 1)
                if not first:
                    pe.wait_ge(lin_biased, n)
                for gl in range(2):
                    for q in range(2):
                        for r in range(2):
                            o = 256 * q + P * r
                            mm = pe.transpose(ps[:, 2 + gl, o:o + P], u_sb[:, q, 256 * r + gl:256 * r + gl + 255:2], ident)
                mm.then_inc(ut_done, 1)

            def down(n, which, first=False):
                pe.wait_ge(h_act, n + 1)
                if not first:
                    pe.wait_ge(y_copied, n)
                for f in range(KF):
                    if f % 2 == 0:
                        pe.wait_ge(w2_in[f // 2], 16 * n + 16)
                    for c in range(2):
                        mm = pe.matmul(ps[64 * c:64 * c + 64, 6, :], hT[:, which, order_of(f), :],
                                       ring[:, 8 + f // 2, D * (f % 2) + 512 * c:D * (f % 2) + 512 * c + 512],
                                       start=(f == 0), stop=(f == KF - 1))
                    if f % 2:
                        mm.then_inc(w2_used, 1)

            def turn_gates(p):
                for which in range(2):
                    if which == 0:
                        pe.wait_ge(gpick_ready, p + 1)
                        pe.wait_ge(xe_ready, 2 * p + 2)
                    else:
                        pe.wait_ge(gpT_copied, 2 * p + 1)
                    for t, (t0, r) in enumerate(TILES):
                        mm = pe.transpose(ps[:, 7, t0:t0 + r], gpick[0:r, t, which, :], ident[0:r, 0:r])
                    mm.then_inc(gpT_done, 1)

            def combine(c, t, biases=False):
                if not (biases and t == 0):
                    pe.wait_ge(comb_added, c)
                t0, r = TILES[t]
                for which in range(1 if biases else 2):
                    for half in range(2):
                        if biases:
                            mm = pe.matmul(ps[0:r, XB + half, :], gateT[:, t0:t0 + r], b2r[:, 512 * half:512 * half + 512],
                                           start=True, stop=True)
                        else:
                            mm = pe.matmul(ps[:, XB + half, :], gpickT[64 * half:64 * half + 64, which, t0:t0 + P],
                                           y_sb[64 * half:64 * half + 64, which, :], start=(which == 0), stop=(which == 1))
                mm.then_inc(comb_done, 1)

            def body(p, first=False, main=False):
                fresh = first and main
                gather(p)
                if not first:
                    down(2 * p - 1, 1)
                up(2 * p, 0, first=fresh)
                if not first:
                    pe.wait_ge(y_copied, 2 * p)
                    combine(3 * p, 0)
                elif main:
                    pe.wait_ge(gT_copied, 1)
                    combine(0, 0, biases=True)
                turn(2 * p, first=fresh)
                up(2 * p + 1, 1)
                for t in (1, 2):
                    if not first:
                        combine(3 * p + t, t)
                    elif main:
                        combine(t, t, biases=True)
                down(2 * p, 0, first=fresh)
                turn_gates(p)
                turn(2 * p + 1)

            def tail(p):
                down(2 * p - 1, 1)
                pe.wait_ge(y_copied, 2 * p)
                for t in range(3):
                    combine(3 * p + t, t)

            HALF = EXPERTS // 2
            pe.wait_ge(h_ready, 3)
            pe.wait_ge(count_ready, 1)
            body(0, first=True, main=True)
            with pe.Fori(1, HALF) as i:
                body(i)
            tail(HALF)
            pe.wait_ge(count_ready, 1)
            busiest = pe.value_load(most[0:1, 0:1], min_val=0, max_val=T)
            with pe.If(busiest > SLOTS):
                with pe.Fori(1, PASSES) as b:
                    body(HALF * b, first=True)
                    with pe.Fori(1, HALF) as i:
                        body(HALF * b + i)
                    tail(HALF * b + HALF)
                pe.nop()
            pe.nop()

        @block.scalar
        def _(act):
            steps = [0]

            def link(ins):
                steps[0] += 1
                ins.then_inc(act_steps, 1)
                act.wait_ge(act_steps, steps[0])

            for t, (_, r) in enumerate(TILES):
                act.wait_ge(x_in, 16 * 3)
                if t == 0:
                    act.wait_ge(rstd_base, 1)
                nc.scalar.activation(xn[0:r, t, :], acc[0:r, t, :], ACT.Square,
                                     accum_out=small[0:r, t:t + 1]).then_inc(ss_ready, 1)
            act.wait_ge(rstd_base, 2)
            nc.scalar.activation(small[:, 8:11], small[:, 4:7], ACT.Sqrt).then_inc(rstd_ready, 1)

            def evacuate(n):
                kind, j = TILE_ORDER[n]
                src = ps[:, n % 3, 0:T]
                act.wait_ge(pj_ready, n + 1)
                if kind in ("q", "k"):
                    b = n % 2
                    if n >= 2:
                        act.wait_ge(qk_done, n - 1)
                    else:
                        act.wait_ge(xn_ready, 3)
                    nc.scalar.activation(squares[:, b, :], src, ACT.Square).then_inc(sq_ready, 1)
                    nc.scalar.copy(raw[:, b, :], src).then_inc(pj_freed, 1)
                elif kind in ("va", "vb"):
                    r = TILES[j][1]
                    if kind == "va":
                        nc.scalar.copy(vA[0:r, j, :], ps[0:r, n % 3, 0:P]).then_inc(pj_freed, 1)
                    else:
                        nc.scalar.copy(vB[0:r, j, :], ps[0:r, n % 3, :]).then_inc(pj_freed, 1)
                elif kind == "qb":
                    nc.scalar.activation(qbT[:, j, :], src, ACT.Copy, scale=SCALE).then_inc(pj_freed, 1)
                elif kind == "kb":
                    nc.scalar.copy(kbT[:, j, :], src).then_inc(pj_freed, 1)
                elif kind == "glow":
                    nc.scalar.copy(glT[:, :], ps[0:RANK, n % 3, 0:T]).then_inc(pj_freed, 1)
                elif kind == "rb":
                    nc.scalar.copy(rbT[:, j, :], src)
                    nc.scalar.activation(rsT[:, j, :], src, ACT.Exp, scale=-1.0).then_inc(pj_freed, 1)
                else:
                    dst = gaT if kind == "ga" else gbT
                    nc.scalar.activation(dst[:, j, :], src, ACT.Exp, scale=-1.0).then_inc(pj_freed, 1)

            def root(j):
                act.wait_ge(var_ready, j + 1)
                nc.scalar.activation(rstd_qk[:, j % 2, :], rstd_qk[:, j % 2, :], ACT.Sqrt).then_inc(qk_rstd, 1)

            def gla_prep():
                act.wait_ge(xy_freed, use(XY_USES, "z"))
                link(nc.scalar.activation(lsp, zb, ACT.Abs))
                link(nc.scalar.activation(lsp, lsp, ACT.Exp, scale=-1.0))
                nc.scalar.activation(lsp, lsp, ACT.Ln, bias=1.0).then_inc(lsp_ready, 1)

            def gla_exps():
                act.wait_ge(decay_ready, 1)
                nc.scalar.activation(q_in, D1, ACT.Exp, scale=1.0 / GATE_NORM)
                nc.scalar.activation(k_in, D1, ACT.Exp, scale=-1.0 / GATE_NORM)
                nc.scalar.activation(q_out, B, ACT.Exp, scale=1.0 / GATE_NORM)
                nc.scalar.activation(k_out, D2, ACT.Exp, scale=-1.0 / GATE_NORM).then_inc(exps_ready, 1)

            def cache_keys():
                act.wait_ge(vw_ready, use(VW_USES, "cache"))
                nc.scalar.copy(ckT.rearrange("p (a b) c -> p a (b c)", a=2), ps[:, VB_:VB_ + 2, :]).then_inc(vw_freed, 1)

            def exps(s):
                act.wait_ge(max_ready, s + 1)
                w0, w1_ = ((P, 256), (P, 256), (0, 256), (0, 256), (0, 192))[s]
                ww = 192 if s == 4 else 256
                for h in range(4):
                    nc.scalar.activation(S_at[:, ww * h + w0:ww * h + w1_], S_at[:, ww * h + w0:ww * h + w1_], ACT.Exp,
                                         bias=small[:, 16 + h:17 + h], accum_out=small[:, 20 + h:21 + h])
                nc.scalar.activation(small[:, 24:28], small[:, 28:32], ACT.Exp).then_inc(exp_done, 1)

            def probs(s):
                act.wait_ge(vw_ready, use(VW_USES, f"probs{s}"))
                if s:
                    act.wait_ge(n_ready, use(N_USES, f"attend{s - 1}"))
                if s < 2:
                    nc.scalar.copy(pT[:, 1, :, :], ps[:, WB, :].rearrange("p (h q) -> p h q", h=4)).then_inc(vw_freed, 1)
                elif s < 4:
                    nc.scalar.copy(pT[:, :, :, :].rearrange("p k h q -> p k (h q)"), ps[:, VB_:VB_ + 2, :]).then_inc(vw_freed, 1)
                else:
                    nc.scalar.copy(pT[:, 0, :, :], ps[:, VB_, :].rearrange("p (h q) -> p h q", h=4))
                    nc.scalar.copy(pT[0:64, 1, :, :], ps[0:64, WB, :].rearrange("p (h q) -> p h q", h=4)).then_inc(vw_freed, 1)

            def gla_prompt_out():
                act.wait_ge(vw_ready, use(VW_USES, "gla_p"))
                act.wait_ge(xy_ready, use(XY_USES, "state3"))
                for a in range(2):
                    out = nc.scalar.copy(obT[:, a::2, 0:PROMPT].rearrange("p j (t q) -> p t j q", t=2),
                                         ps[:, VB_ + a, :].rearrange("p (t j q) -> p t j q", t=2, j=2))
                out.then_inc(vw_freed, 1)

            def gla_sample_out():
                act.wait_ge(vw_ready, use(VW_USES, "gla_s"))
                for a in range(2):
                    out = nc.scalar.copy(obT[:, a::2, PROMPT:T], ps[:, VB_ + a, 0:P].rearrange("p (j q) -> p j q", j=2))
                out.then_inc(vw_freed, 1)

            for n in range(FIRST_RB):
                evacuate(n)
                if 1 <= n <= 5:
                    root(n - 1)
            after = {
                0: [gla_prep, cache_keys],
                1: [gla_exps],
                2: [lambda: exps(0)],
                4: [lambda: probs(0)],
                5: [lambda: exps(1)],
                6: [lambda: probs(1)],
                7: [lambda: exps(2)],
                8: [lambda: probs(2)],
                9: [lambda: exps(3)],
                10: [lambda: probs(3)],
                11: [lambda: exps(4)],
                12: [lambda: probs(4)],
                17: [gla_prompt_out],
                19: [gla_sample_out],
            }
            for s in range(20):
                evacuate(FIRST_RB + s)
                for step in after.get(s, ()):
                    step()
            act.wait_ge(vw_freed, use(VW_USES, "gla_s"))
            act.wait_ge(pj_ready, len(TILE_ORDER))
            nc.scalar.activation(squares_o, obT, ACT.Square).then_inc(sqo_ready, 1)
            act.wait_ge(varo_ready, 1)
            nc.scalar.activation(rstd_o, rstd_o, ACT.Sqrt).then_inc(rstdo_ready, 1)
            for t, (_, r) in enumerate(TILES):
                act.wait_ge(h_ready, t + 1)
                act.wait_ge(mg_ready, 2 * KD)
                nc.scalar.activation(hn[0:r, t, :], acc[0:r, t, :], ACT.Square,
                                     accum_out=small[0:r, 44 + t:45 + t]).then_inc(ss2_ready, 1)
                act.wait_ge(base2_ready, t + 1)
                nc.scalar.activation(small[0:r, 52 + t:53 + t], small[0:r, 48 + t:49 + t], ACT.Sqrt).then_inc(rstd2_ready, 1)
            for t, (_, r) in enumerate(TILES):
                act.wait_ge(top_ready, t + 1)
                nc.scalar.activation(top_e[0:r, :], top8[0:r, 0:4], ACT.Exp, bias=small[0:r, 56:57],
                                     accum_out=small[0:r, 57:58]).then_inc(gexp_ready, 1)

            def copy_u(n, first=False):
                act.wait_ge(w1_used, KD * n + KD)
                if not first:
                    act.wait_ge(ut_done, n)
                nc.scalar.copy(u_sb[:, :, :], ps[:, 0:2, :]).then_inc(u_copied, 1)

            def gate_sigmoid(n, first=False):
                act.wait_ge(glu_ready, n + 1)
                if not first:
                    act.wait_ge(h_act, n)
                nc.scalar.activation(sig, glu, ACT.Sigmoid, scale=1.702).then_inc(sig_ready, 1)

            def copy_y(n, which, combined):
                act.wait_ge(w2_used, 4 * n + 4)
                act.wait_ge(comb_done, combined)
                nc.scalar.copy(y_sb[:, which, :], ps[:, 6, :]).then_inc(y_copied, 1)

            def copy_gates(p):
                for which in range(2):
                    act.wait_ge(gpT_done, 2 * p + which + 1)
                    act.wait_ge(comb_done, 3 * p + 3)
                    nc.scalar.copy(gpickT[:, which, 0:T], ps[:, 7, 0:T]).then_inc(gpT_copied, 1)

            def body(p, first=False, main=False):
                if not first:
                    copy_y(2 * p - 1, 1, 3 * p)
                copy_u(2 * p, first=first and main)
                gate_sigmoid(2 * p, first=first and main)
                copy_u(2 * p + 1)
                copy_y(2 * p, 0, 3 * p + 3)
                copy_gates(p)
                gate_sigmoid(2 * p + 1)

            HALF = EXPERTS // 2
            body(0, first=True, main=True)
            with act.Fori(1, HALF) as i:
                body(i)
            copy_y(EXPERTS - 1, 1, 3 * HALF)
            act.wait_ge(count_ready, 1)
            busiest = act.value_load(most[0:1, 0:1], min_val=0, max_val=T)
            with act.If(busiest > SLOTS):
                with act.Fori(1, PASSES) as b:
                    body(HALF * b, first=True)
                    with act.Fori(1, HALF) as i:
                        body(HALF * b + i)
                    copy_y(EXPERTS * b + EXPERTS - 1, 1, 3 * (HALF * b + HALF))
                act.nop()
            act.nop()

        @block.vector
        def _(dve):
            steps = [0]

            def link(ins):
                steps[0] += 1
                ins.then_inc(dve_steps, 1)
                dve.wait_ge(dve_steps, steps[0])

            def wide(ap, shape):
                return ap.broadcast_to(shape)

            dve.memset(small[:, 0:3], 1.0).then_inc(rstd_base, 1)
            dve.wait_ge(ss_ready, 3)
            link(dve.tensor_scalar(small[:, 4:7], small[:, 0:3], 1.0 / D, NORM_EPS, ALU.mult, ALU.add))
            dve.reciprocal(small[:, 4:7], small[:, 4:7]).then_inc(rstd_base, 1)
            dve.wait_ge(rstd_ready, 1)
            for t, (_, r) in enumerate(TILES):
                dve.tensor_scalar(xn[0:r, t, :], acc[0:r, t, :], small[0:r, 8 + t:9 + t], None, ALU.mult
                                  ).then_inc(xn_ready, 1)
            dve.wait_ge(n_ready, use(N_USES, "rows"))
            dve.tensor_copy(cols[:, :], ps[:, NB, 0:21]).then_inc(n_freed, 1)
            dve.wait_ge(n_freed, use(N_USES, "rows"))
            for t, (t0, r) in enumerate(TILES):
                for half in range(2):
                    u = 2 * t + half
                    dve.wait_ge(xT_ready, u + 1)
                    dve.tensor_tensor(xnT[:, 4 * half:4 * half + 4, t0:t0 + r],
                                      ps[:, XB + u % 4, :].rearrange("p (k q) -> p k q", k=4)[:, :, 0:r],
                                      wide(cols[:, 4 * half:4 * half + 4].unsqueeze(2), [P, 4, r]), ALU.mult
                                      ).then_inc(xnT_ready, 1)
            dve.wait_ge(n_ready, use(N_USES, "b1"))
            dve.tensor_copy(b1T[:, :, :, :].rearrange("p e g f -> p (g f) e"),
                            ps[:, NB, :].rearrange("p (c e) -> p c e", e=EXPERTS)).then_inc(n_freed, 1)
            dve.wait_ge(small_in, 16 * 6)
            dve.wait_ge(consts_in, 16)
            for i in range(2):
                dve.tensor_copy(sinkr[:, i, :].rearrange("p (g j) -> p g j", g=KVH),
                                sinkc[:, :].rearrange("p (g h) -> p g h", g=KVH)[:, :, 2 * i:2 * i + 2])
            link(dve.tensor_tensor(sink_s[:, :, :], sinkc[:, :].rearrange("p (g h) -> p g h", g=KVH),
                                   wide(const("head_of").unsqueeze(1), [P, KVH, GROUP]), ALU.mult))
            link(dve.tensor_reduce(small[:, 36:38], sink_s[:, :, :], AX.X, ALU.add))
            link(dve.tensor_copy(sinkr[:, 2, :].rearrange("p (g h) -> p g h", g=KVH),
                                 wide(small[:, 36:38].unsqueeze(2), [P, KVH, 2])))
            for j in range(5):
                b = j % 2
                dve.wait_ge(n_ready, use(N_USES, f"norm{j}"))
                if j >= 2:
                    dve.wait_ge(qk_done, j - 1)
                dve.tensor_scalar(rstd_qk[:, b, :], ps[:, NB, 0:T], QK_EPS, None, ALU.add).then_inc(n_freed, 1)
                dve.wait_ge(n_freed, use(N_USES, f"norm{j}"))
                dve.reciprocal(rstd_qk[:, b, :], rstd_qk[:, b, :]).then_inc(var_ready, 1)
                dve.wait_ge(qk_rstd, j + 1)
                dve.wait_ge(pj_freed, j + 1)
                if j < 4:
                    dve.scalar_tensor_tensor(qT[:, j, :], raw[:, b, 0:PROMPT], cols[:, 18:19], rstd_qk[:, b, 0:PROMPT],
                                             ALU.mult, ALU.mult)
                    dve.scalar_tensor_tensor(qS[:, :, j, :], raw[:, b, PROMPT:T].rearrange("p (b t) -> p b t", t=TSEQ),
                                             cols[:, 18:19], rstd_qk[:, b, PROMPT:T].rearrange("p (b t) -> p b t", t=TSEQ),
                                             ALU.mult, ALU.mult).then_inc(qk_done, 1)
                else:
                    dve.scalar_tensor_tensor(kT[:, :], raw[:, b, :], cols[:, 19:20], rstd_qk[:, b, :],
                                             ALU.mult, ALU.mult).then_inc(qk_done, 1)

            dve.wait_ge(xy_ready, use(XY_USES, "z"))
            for j in range(PAIRS):
                last = dve.tensor_scalar(zb[:, j, :], ps[:, XB + j, 0:T], cols[:, 16 + j:17 + j], None, ALU.add)
            last.then_inc(xy_freed, 1)
            dve.wait_ge(xy_freed, use(XY_USES, "z"))
            dve.wait_ge(lsp_ready, 1)
            link(dve.scalar_tensor_tensor(zb, zb, 0.0, lsp, ALU.min, ALU.subtract))
            for j in range(PAIRS):
                scan = dve.tensor_tensor_scan(B[:, j, :], const("keep"), zb[:, j, :], 0.0, ALU.mult, ALU.add)
            link(scan)
            for first, end, c in ((0, PROMPT, CHUNK), (PROMPT, T, TSEQ)):
                b4 = B[:, :, first:end].rearrange("p j (n c) -> p j n c", c=c)
                shape = [P, PAIRS, (end - first) // c, c]
                for dst, at in ((D1, c // 2 - 1), (D2, c - 1)):
                    last = dve.tensor_tensor(dst[:, :, first:end].rearrange("p j (n c) -> p j n c", c=c), b4,
                                             wide(b4[:, :, :, at:at + 1], shape), ALU.subtract)
            last.then_inc(decay_ready, 1)

            dve.wait_ge(n_ready, use(N_USES, "keys"))
            dve.tensor_copy(kTok[:, 0, :], ps[:, NB, 0:P])
            dve.tensor_copy(kTok[0:64, 1, :], ps[0:64, NB, P:2 * P]).then_inc(n_freed, 1)

            dve.wait_ge(exps_ready, 1)
            dve.tensor_copy(dec[:, :, 0:NCH], q_out[:, :, CHUNK - 1:PROMPT:CHUNK])
            link(dve.tensor_copy(dec[:, :, NCH:], q_out[:, :, PROMPT + TSEQ - 1:T:TSEQ]))
            dve.tensor_tensor(q_in, q_in, qbT[:, :, :], ALU.mult)
            dve.tensor_tensor(k_in, k_in, kbT[:, :, :], ALU.mult)
            dve.tensor_tensor(q_out, q_out, qbT[:, :, :], ALU.mult)
            dve.tensor_tensor(k_out, k_out, kbT[:, :, :], ALU.mult).then_inc(gla_ops, 1)

            def softmax_max(s):
                dve.wait_ge(xy_ready, use(XY_USES, f"scores{s}"))
                if s:
                    dve.wait_ge(vw_ready, use(VW_USES, f"probs{s - 1}"))
                for g in range(KVH):
                    bank = ps[:, XB + g, :]
                    if s < 4:
                        w = 256 if s >= 2 else P
                        out = S_at[:, 512 * g:512 * g + 512].rearrange("p (h c) -> p h c", h=2)[:, :, 256 - w:256]
                        last = dve.scalar_tensor_tensor(
                            out, bank.rearrange("p (h c) -> p h c", h=2)[:, :, 0:w], SCALE,
                            wide(const("band")[:, 256 - w:256].unsqueeze(1), [P, 2, w]), ALU.mult, ALU.add)
                    else:
                        last = dve.scalar_tensor_tensor(S_at[:, 384 * g:384 * g + 384], bank[:, 0:384], SCALE,
                                                        const("sample_mask"), ALU.mult, ALU.add)
                last.then_inc(xy_freed, 1)
                dve.wait_ge(xy_freed, use(XY_USES, f"scores{s}"))
                all_s = probs_of(s)
                sink = sinkr[:, 2 if s == 4 else s % 2, :]
                link(dve.tensor_reduce(small[:, 12:16], all_s, AX.X, ALU.max))
                link(dve.tensor_tensor(small[:, 12:16], small[:, 12:16], sink, ALU.max))
                dve.tensor_scalar(small[:, 16:20], small[:, 12:16], -1.0, None, ALU.mult)
                dve.tensor_tensor(small[:, 28:32], sink, small[:, 12:16], ALU.subtract).then_inc(max_ready, 1)

            def probs_of(s):
                if s == 4:
                    return S_at[:, 0:768].rearrange("p (h c) -> p h c", h=4)
                return S_at.rearrange("p (h c) -> p h c", h=4)[:, :, (0 if s >= 2 else P):256]

            def softmax_norm(s):
                dve.wait_ge(exp_done, s + 1)
                all_s = probs_of(s)
                w = (P, P, 256, 256, 192)[s]
                link(dve.tensor_tensor(small[:, 20:24], small[:, 20:24], small[:, 24:28], ALU.add))
                link(dve.reciprocal(small[:, 32:36], small[:, 20:24]))
                dve.tensor_tensor(all_s, all_s, wide(small[:, 32:36].unsqueeze(2), [P, 4, w]), ALU.mult
                                  ).then_inc(p_ready, 1)

            def attended(s):
                dve.wait_ge(n_ready, use(N_USES, f"attend{s}"))
                if s < 4:
                    n, i = divmod(s, 2)
                    dve.tensor_copy(oT[:, 2 * i:2 * i + 2, P * n:P * n + P],
                                    ps[:, NB, 0:256].rearrange("p (j q) -> p j q", j=2)).then_inc(n_freed, 1)
                else:
                    dve.tensor_copy(oT[:, :, PROMPT:T].rearrange("p j (b t) -> p b j t", t=TSEQ),
                                    ps[:, NB, 0:256].rearrange("p (b j t) -> p b j t", b=NSEQ, j=4)).then_inc(n_freed, 1)

            def mask_decays_prompt():
                dve.wait_ge(xy_ready, use(XY_USES, "decays_p"))
                for a in range(2):
                    last = dve.tensor_tensor(AT_p[:, a, :, :, :].rearrange("p t j s -> p (t j) s"),
                                             ps[:, XB + a, :].rearrange("p (c s) -> p c s", c=4),
                                             wide(const("gla_mask").unsqueeze(1), [P, 4, P]), ALU.mult)
                last.then_inc(xy_freed, 1)

            def mask_decays_sample():
                dve.memset(AT_s[64:128, :, :, :], 0.0)
                dve.wait_ge(xy_ready, use(XY_USES, "decays_s"))
                for a in range(2):
                    last = dve.tensor_tensor(AT_s[0:64, a, :, :],
                                             ps[0:64, XB + a, 0:P].rearrange("p (c s) -> p c s", c=2),
                                             wide(const("gla_smask", 64).unsqueeze(1), [64, 2, 64]), ALU.mult)
                last.then_inc(xy_freed, 1)

            def mask_keys(t):
                dve.wait_ge(n_ready, use(N_USES, f"gkeys{t}"))
                if t == 1:
                    dve.wait_ge(xy_ready, use(XY_USES, "state0"))
                r = TILES[t][1]
                count, dst, which = ((CPT, kM, "chunk_of"), (NSEQ, kMs[0:64, :, :], "seq_of"))[t == 2]
                dve.tensor_tensor(dst, wide(ps[0:r, NB, 0:256].unsqueeze(1), [r, count, 256]),
                                  wide(const(which, r).unsqueeze(2), [r, count, 256]), ALU.mult).then_inc(n_freed, 1)

            def step_states(which):
                dve.wait_ge(xy_ready, use(XY_USES, f"state{which}"))
                if which == 2:
                    dve.wait_ge(s0_in, 16)
                for c in range(4):
                    for j in range(PAIRS):
                        update = ps[:, XB + c // 2, 256 * (c % 2) + P * j:256 * (c % 2) + P * j + P]
                        if which < 2:
                            n = 4 * which + c
                            if n == 0:
                                last = dve.tensor_copy(S_all[:, 1, j, :], update)
                            else:
                                last = dve.scalar_tensor_tensor(S_all[:, n + 1, j, :], S_all[:, n, j, :],
                                                                dec[:, j, n:n + 1], update, ALU.mult, ALU.add)
                        else:
                            b = 4 * (which - 2) + c
                            last = dve.scalar_tensor_tensor(S_new[:, b, j, :], S0[:, b, j, :],
                                                            dec[:, j, NCH + b:NCH + b + 1], update, ALU.mult, ALU.add)
                    if which < 2 and c < 3:
                        link(last)
                last.then_inc(xy_freed, 1)
                if which == 0:
                    dve.wait_ge(xy_freed, use(XY_USES, "state0"))

            def sigmoid(x):
                link(dve.tensor_scalar(x[:, :, :], x[:, :, :], 1.0, None, ALU.add))
                link(dve.reciprocal(x[:, :, :], x[:, :, :]))

            softmax_max(0)
            for s in range(4):
                softmax_norm(s)
                softmax_max(s + 1)
                attended(s)
            softmax_norm(4)
            mask_decays_prompt()
            attended(4)
            mask_decays_sample()
            mask_keys(0)
            step_states(0)
            dve.wait_ge(pj_freed, tiles_done("ga", 7))
            sigmoid(gaT)
            mask_keys(1)
            step_states(1)
            mask_keys(2)
            step_states(2)
            sigmoid(rsT)
            step_states(3)
            link(dve.tensor_tensor(rbT[:, :, :], rbT[:, :, :], rsT[:, :, :], ALU.mult))
            dve.wait_ge(pj_freed, tiles_done("gb", 7))
            sigmoid(gbT)

            def merge_a(m):
                dve.wait_ge(mg_ready, m + 1)
                dve.tensor_tensor(gaT[:, m, :], gaT[:, m, :], ps[:, m % 3, 0:T], ALU.mult).then_inc(mg_freed, 1)

            for m in range(4):
                merge_a(m)
            for h in range(GH):
                dve.wait_ge(n_ready, use(N_USES, f"dv{h}"))
                dve.tensor_scalar(rstd_o[:, h, :], ps[:, NB, 0:T], NORM_EPS, None, ALU.add).then_inc(n_freed, 1)
            dve.wait_ge(n_freed, len(N_USES))
            dve.reciprocal(rstd_o, rstd_o).then_inc(varo_ready, 1)
            for m in range(4, KD):
                merge_a(m)
            dve.wait_ge(rstdo_ready, 1)
            link(dve.scalar_tensor_tensor(obT, obT, cols[:, 20:21], rstd_o, ALU.mult, ALU.mult))
            dve.tensor_tensor(obT, obT, rbT[:, :, :], ALU.mult).then_inc(ob_done, 1)
            for m in range(KD):
                u = KD + m
                dve.wait_ge(mg_ready, u + 1)
                dve.tensor_tensor(gbT[:, m, :], gbT[:, m, :], ps[:, u % 3, 0:T], ALU.mult).then_inc(mg_freed, 1)
                dve.wait_ge(mg_freed, u + 1)
                dve.tensor_tensor(xnT[:, m, :], gaT[:, m, :], gbT[:, m, :], ALU.add).then_inc(merged_ready, 1)
            dve.wait_ge(x_again, 48)
            for t, (_, r) in enumerate(TILES):
                bank = (XB, VB_, XB)[t]
                dve.wait_ge(h_psum, t + 1)
                dve.tensor_tensor(acc[0:r, t, :], acc[0:r, t, :],
                                  ps[0:r, bank:bank + 2, :].rearrange("p a b -> p (a b)"), ALU.add).then_inc(h_ready, 1)
                dve.wait_ge(ss2_ready, t + 1)
                link(dve.tensor_scalar(small[0:r, 48 + t:49 + t], small[0:r, 44 + t:45 + t], 1.0 / D, NORM_EPS,
                                       ALU.mult, ALU.add))
                dve.reciprocal(small[0:r, 48 + t:49 + t], small[0:r, 48 + t:49 + t]).then_inc(base2_ready, 1)
                dve.wait_ge(rstd2_ready, t + 1)
                dve.tensor_scalar(hn[0:r, t, :], acc[0:r, t, :], small[0:r, 52 + t:53 + t], None, ALU.mult
                                  ).then_inc(hn_ready, 1)

            def routed(t):
                t0, r = TILES[t]
                dve.wait_ge(hnT_psum, t + 1)
                dve.tensor_tensor(hnT[:, :, t0:t0 + r],
                                  ps[:, 0:2, :].rearrange("p a (k q) -> p (a k) q", k=4)[:, :, 0:r],
                                  wide(cols[:, 8:16].unsqueeze(2), [P, KD, r]), ALU.mult).then_inc(hnT_ready, 1)
                dve.wait_ge(lg_psum, t + 1)
                dve.tensor_tensor(lg[0:r, :], ps[0:r, 2, 0:EXPERTS], b_rt[0:r, :], ALU.add).then_inc(lgt_freed, 1)
                dve.wait_ge(lgt_freed, t + 1)
                link(dve.max(top8[0:r, :], lg[0:r, :]))
                link(dve.max_index(idx8[0:r, :], top8[0:r, :], lg[0:r, :]))
                link(dve.tensor_copy(idxf[0:r, :], idx8[0:r, 0:4]))
                dve.tensor_scalar(small[0:r, 56:57], top8[0:r, 0:1], -1.0, None, ALU.mult).then_inc(top_ready, 1)
                link(dve.tensor_tensor(onehot[0:r, :, :], wide(const("expert", r).unsqueeze(1), [r, TOPK, EXPERTS]),
                                       wide(idxf[0:r, :].unsqueeze(2), [r, TOPK, EXPERTS]), ALU.is_equal))
                dve.tensor_reduce(sel[0:r, t, :], onehot[0:r, :, :].rearrange("p k e -> p e k"), AX.X, ALU.add)
                dve.wait_ge(gexp_ready, t + 1)
                link(dve.reciprocal(small[0:r, 58:59], small[0:r, 57:58]))
                link(dve.tensor_scalar(top_e[0:r, :], top_e[0:r, :], small[0:r, 58:59], None, ALU.mult))
                link(dve.tensor_tensor(onehot_g[0:r, :, :], onehot[0:r, :, :],
                                       wide(top_e[0:r, :].unsqueeze(2), [r, TOPK, EXPERTS]), ALU.mult))
                dve.tensor_reduce(gates[0:r, t, 0:EXPERTS], onehot_g[0:r, :, :].rearrange("p k e -> p e k"), AX.X, ALU.add
                                  ).then_inc(route_ready, 1)

            dve.wait_ge(pads_ready, 4)
            dve.wait_ge(small_in, 16 * 6)
            for t in range(3):
                routed(t)
            dve.wait_ge(pos_psum, 1)
            for t, (_, r) in enumerate(TILES):
                last = dve.scalar_tensor_tensor(place[0:r, t, 0:EXPERTS], ps[0:r, NB, EXPERTS * t:EXPERTS * (t + 1)], 1.0,
                                                sel[0:r, t, :], ALU.add, ALU.mult)
            link(last)
            for t, (_, r) in enumerate(TILES):
                last = dve.tensor_scalar(place[0:r, t, 0:EXPERTS], place[0:r, t, 0:EXPERTS], -1.0, None, ALU.add)
            link(last)
            link(dve.tensor_reduce(small[0:1, 60:61], ps[0:1, NB, 96:128], AX.X, ALU.max))
            dve.tensor_copy(most[:, :], small[0:1, 60:61]).then_inc(count_ready, 1)

            def pick_tokens(p, e, fresh=False):
                if not fresh:
                    dve.wait_ge(gather_done, 2 * p)
                for which in range(2):
                    for t, (_, r) in enumerate(TILES):
                        last = dve.tensor_scalar(pick[0:r, t, SLOTS * which:SLOTS * (which + 1)],
                                                 const("slot", r)[:, 0:SLOTS], place[0:r, t, bass.ds(e + which, 1)], None,
                                                 ALU.is_equal)
                last.then_inc(pick_ready, 1)

            def pick_gates(p, e, fresh=False):
                if not fresh:
                    dve.wait_ge(gpT_done, 2 * p)
                for which in range(2):
                    for t, (_, r) in enumerate(TILES):
                        last = dve.tensor_scalar(gpick[0:r, t, which, :], const("slot", r),
                                                 place[0:r, t, bass.ds(e + which, 1)],
                                                 gates[0:r, t, bass.ds(e + which, 1)], ALU.is_equal, ALU.mult)
                last.then_inc(gpick_ready, 1)

            def take_tokens(p, fresh=False):
                if not fresh:
                    dve.wait_ge(w1_used, 2 * KD * p)
                for half in range(2):
                    dve.wait_ge(gather_done, 2 * p + half + 1)
                    dve.tensor_tensor(xeT[:, 4 * half:4 * half + 4, :], ps[:, 7, :].rearrange("p (k s) -> p k s", k=4),
                                      wide(cols[:, 8 + 4 * half:12 + 4 * half].unsqueeze(2), [P, 4, P]), ALU.mult
                                      ).then_inc(xe_ready, 1)

            def swiglu(n, e, which, fresh=False):
                dve.wait_ge(ut_done, n + 1)
                if not fresh:
                    dve.wait_ge(h_act, n)
                dve.tensor_tensor(glu, ps[:, 2, :].rearrange("p (f t) -> p f t", f=KF),
                                  wide(b1T[:, bass.ds(e, 1), 0, :].rearrange("p a f -> p (a f)").unsqueeze(2), [P, KF, SLOTS]),
                                  ALU.add).then_inc(glu_biased, 1)
                dve.wait_ge(glu_biased, n + 1)
                dve.tensor_scalar(glu, glu, 7.0, None, ALU.min).then_inc(glu_ready, 1)
                dve.tensor_tensor(lin, ps[:, 3, :].rearrange("p (f t) -> p f t", f=KF),
                                  wide(b1T[:, bass.ds(e, 1), 1, :].rearrange("p a f -> p (a f)").unsqueeze(2), [P, KF, SLOTS]),
                                  ALU.add).then_inc(lin_biased, 1)
                dve.wait_ge(lin_biased, n + 1)
                dve.tensor_scalar(lin, lin, 7.0, -7.0, ALU.min, ALU.max).then_inc(lin_ready, 1)
                dve.wait_ge(lin_ready, n + 1)
                dve.scalar_tensor_tensor(lin, lin, 1.0, glu, ALU.add, ALU.mult).then_inc(prod_ready, 1)
                dve.wait_ge(prod_ready, n + 1)
                dve.wait_ge(sig_ready, n + 1)
                if not fresh:
                    dve.wait_ge(w2_used, 4 * (n - 1))
                dve.tensor_tensor(hT[:, which, :, :], lin, sig, ALU.mult).then_inc(h_act, 1)

            def add(c, t):
                r = TILES[t][1]
                dve.wait_ge(comb_done, c + 1)
                dve.tensor_tensor(acc[0:r, t, :], acc[0:r, t, :],
                                  ps[0:r, XB:XB + 2, :].rearrange("p a b -> p (a b)"), ALU.add).then_inc(comb_added, 1)

            def body(p, i, first=False, main=False, last=False):
                fresh = first and main
                take_tokens(p, fresh)
                pick_gates(p, 2 * i, fresh)
                if not first or main:
                    add(3 * p, 0)
                swiglu(2 * p, 2 * i, 0, fresh)
                if not first or main:
                    add(3 * p + 1, 1)
                    add(3 * p + 2, 2)
                if not last:
                    pick_tokens(p + 1, 2 * i + 2)
                swiglu(2 * p + 1, 2 * i + 1, 1)

            def tail(p):
                for t in range(3):
                    add(3 * p + t, t)

            HALF = EXPERTS // 2
            pick_tokens(0, 0, fresh=True)
            dve.memset(gpickT[:, :, T:], 0.0)
            dve.wait_ge(pos_psum, 2)
            dve.tensor_copy(gateT[:, :], ps[0:EXPERTS, 2, 0:T]).then_inc(gT_copied, 1)
            body(0, 0, first=True, main=True)
            with dve.Fori(1, HALF - 1) as i:
                body(i, i)
            body(HALF - 1, HALF - 1, last=True)
            tail(HALF)
            busiest = dve.value_load(most[0:1, 0:1], min_val=0, max_val=T)
            with dve.If(busiest > SLOTS):
                with dve.Fori(1, PASSES) as b:
                    dve.tensor_scalar(const("slot"), const("slot"), float(SLOTS), None, ALU.add).then_inc(slots_moved, 1)
                    dve.wait_ge(slots_moved, b)
                    pick_tokens(HALF * b, 0)
                    body(HALF * b, 0, first=True)
                    with dve.Fori(1, HALF - 1) as i:
                        body(HALF * b + i, i)
                    body(HALF * b + HALF - 1, HALF - 1, last=True)
                    tail(HALF * b + HALF)
                dve.wait_ge(comb_added, 3 * (HALF * PASSES + 1))
            dve.wait_ge(comb_added, 3 * (HALF + 1))
            dve.tensor_copy(small[0:1, 61:62], small[0:1, 60:61]).then_inc(acc_final, 1)


_INS = ["x_prompt", "x_sample", "cache_swa_k", "cache_swa_v", "state_gla", "norm1", "w_in", "q_norm", "k_norm",
        "sinks", "w_gk", "b_gk", "gla_norm", "w_a", "w_b", "w_o", "norm2", "w_router", "b_router", "w1", "b1",
        "w2", "b2"]
_OUTS = [(1, 256, 1024), (8, 8, 1024), (1, 1, 128, 2, 64), (1, 1, 128, 2, 64), (1, 1, 4, 64, 128),
         (1, 8, 128, 2, 64), (1, 8, 128, 2, 64), (1, 8, 4, 64, 128)]


def kernel(**inputs):
    import concourse.bacc as bacc
    from concourse.bass_utils import run_bass_kernel_spmd

    nc = bacc.Bacc("TRN2", target_bir_lowering=False, num_devices=1)
    arrays, args = {}, []
    for name in _INS + ["consts"]:
        a = constants() if name == "consts" else np.ascontiguousarray(inputs[name])
        arrays[f"in_{name}"] = a
        args.append(nc.dram_tensor(f"in_{name}", a.shape, mybir.dt.from_np(a.dtype), kind="ExternalInput").ap())
    for i, shape in enumerate(_OUTS):
        args.append(nc.dram_tensor(f"out_{i}", shape, F32, kind="ExternalOutput").ap())
    layer(nc, *args)
    r = run_bass_kernel_spmd(nc, [arrays], core_ids=[0])
    return tuple(r.results[0][f"out_{i}"] for i in range(len(_OUTS)))
```

```python
from contextlib import ExitStack

import numpy as np

import concourse.bass as bass
from concourse import mybir

F32 = mybir.dt.float32
I32 = mybir.dt.int32
U32 = mybir.dt.uint32
ALU = mybir.AluOpType
ACT = mybir.ActivationFunctionType
AX = mybir.AxisListType

P = 128
D = 1024
KD = D // P
PROMPT, NSEQ, TSEQ = 256, 8, 8
T = PROMPT + NSEQ * TSEQ
TILES = [(0, 128), (128, 128), (256, 64)]
HEADS, KVH, HD = 8, 2, 64
GROUP = HEADS // KVH
GH, GDK, GDV, RANK = 4, 64, 128, 16
PAIRS = GH // 2
CHUNK = 32
NCH = PROMPT // CHUNK
CPT = P // CHUNK
EXPERTS, TOPK, FF = 32, 4, 1024
EARLY = 2
SLOTS = 64
PASSES = T // SLOTS
KF = FF // P
NORM_EPS, QK_EPS, NEG = 1e-5, 1e-6, -1e30
SCALE = 0.125
GATE_NORM = 16.0

C_Q, C_K, C_V, C_QB, C_KB, C_VB = 0, 512, 640, 768, 1024, 1280
C_GLOW, C_RB, C_GA, C_GB = 1792, 1808, 2320, 3344
UNIT = 256
W_UNITS = [C_K, C_QB, C_KB, C_VB, C_VB + UNIT] + [C_RB + UNIT * i for i in range(2)] \
    + [C_GA + UNIT * i for i in range(4)] + [C_GB + UNIT * i for i in range(4)]
NU = 2 + len(W_UNITS)
RING = 12
FIRST_SLOT, STREAM_SLOTS = 6, 6

TILE_ORDER = [("q", j) for j in range(4)] + [("k", 0)] + [("va", t) for t in range(3)] \
    + [("qb", j) for j in range(2)] + [("kb", j) for j in range(2)] + [("glow", 0)] \
    + [("vb", t) for t in range(3)] + [("rb", j) for j in range(4)] \
    + [("ga", j) for j in range(8)] + [("gb", j) for j in range(8)]
FIRST_RB = 16

N_USES = ["n1_column", "vectors"] + [f"norm{j}" for j in range(5)] + ["b1", "keys"] + [f"attend{s}" for s in range(5)] \
    + [f"gkeys{t}" for t in range(3)] + [f"dv{h}" for h in range(GH)]
XY_USES = ["z"] + [f"scores{s}" for s in range(5)] + ["decays_p", "decays_s"] + [f"state{w}" for w in range(4)]
VW_USES = ["cache"] + [f"probs{s}" for s in range(5)] + ["gla_p", "gla_s"]


def use(uses, name):
    return uses.index(name) + 1


def tiles_done(kind, j):
    return TILE_ORDER.index((kind, j)) + 1


def unit_done(m):
    last = [("q", 1), ("q", 3), ("va", 2), ("qb", 1), ("kb", 1), ("vb", 2), ("vb", 2)]
    return tiles_done(*last[m]) if m < len(last) else FIRST_RB + 2 * (m - 6)


CONST_AT, _at = {}, 0
for _name, _w in [("ident", 128), ("head_mean", 128), ("dv_mean", 128), ("before", 128), ("ones", 128),
                  ("band", 256), ("sample_mask", 384), ("gla_mask", 128), ("gla_smask", 64),
                  ("chunk_of", 4), ("seq_of", 8), ("head_of", 4), ("keep", 320), ("slot", 128),
                  ("expert", 32)]:
    CONST_AT[_name] = (_at, _w)
    _at += _w
NCONST = _at


def constants():
    c = {n: np.zeros((P, w), np.float32) for n, (_, w) in CONST_AT.items()}
    p = np.arange(P)
    c["ident"][:] = np.eye(P)
    c["head_mean"][:] = (p[:, None] // HD == p[None] // HD) / HD
    c["dv_mean"][:] = 1.0 / GDV
    c["before"][:] = p[:, None] < p[None]
    c["ones"][:] = 1.0
    key = np.arange(2 * P)[None]
    c["band"][:] = np.where((key > p[:, None]) & (key <= p[:, None] + P), 0.0, NEG)
    seq, tok = p // 32, p % 8
    for half in range(2):
        key = np.arange(P)[None]
        old = key > tok[:, None]
        new = np.arange(NSEQ * TSEQ)[None]
        new = (new // TSEQ == (4 * half + seq)[:, None]) & (new % TSEQ <= tok[:, None])
        c["sample_mask"][:, 192 * half:192 * half + 192] = np.where(np.concatenate([old, new], 1), 0.0, NEG)
    c["gla_mask"][:] = (p[:, None] // CHUNK == p[None] // CHUNK) & (p[:, None] <= p[None])
    s = np.arange(64)
    c["gla_smask"][:64] = (s[:, None] // TSEQ == s[None] // TSEQ) & (s[:, None] <= s[None])
    c["chunk_of"][:] = p[:, None] // CHUNK == np.arange(4)[None]
    c["seq_of"][:] = p[:, None] // TSEQ == np.arange(8)[None]
    c["head_of"][:] = p[:, None] % 32 // 8 == np.arange(4)[None]
    t = np.arange(T)
    c["keep"][:] = np.where(t < PROMPT, t % CHUNK != 0, t % TSEQ != 0)
    c["slot"][:] = 1 + np.arange(P) % SLOTS
    c["expert"][:] = np.arange(EXPERTS)
    return np.concatenate([c[n] for n in CONST_AT], 1)


def layer(nc: bass.Bass, x_prompt, x_sample, cache_k, cache_v, state_gla, norm1, w_in, q_norm, k_norm,
          sinks, w_gk, b_gk, gla_norm, w_a, w_b, w_o, norm2, w_router, b_router, w1, b1, w2, b2, consts,
          y_prompt, y_sample, k_prompt, v_prompt, s_prompt, k_sample, v_sample, s_sample):
    with ExitStack() as ctx:
        def sb(name, shape, dt=F32):
            return ctx.enter_context(nc.sbuf_tensor(name, shape, dt))

        def sem(name):
            return ctx.enter_context(nc.semaphore(name))

        ring = sb("ring", [P, RING, 2048])
        cst = sb("cst", [P, NCONST])
        acc = sb("acc", [P, 3, D])
        region2 = sb("region2", [P, 3 * D])
        xnT = sb("xnT", [P, KD, T])
        region_kv = sb("region_kv", [P, 2304 + T + 3 * GH * GDV])
        region_q = region_kv[:, 0:2304]
        kT = region_kv[:, 2304:2304 + T]
        vB = region_kv[:, 2304 + T:].rearrange("p (t c) -> p t c", t=3)
        early = region_kv[:, 0:EARLY * 2048].rearrange("p (k c) -> p k c", k=EARLY)
        qbT = sb("qbT", [P, PAIRS, T])
        kbT = sb("kbT", [P, PAIRS, T])
        vA = sb("vA", [P, 3, P])
        rbT = sb("rbT", [P, GH, T])
        rsT = sb("rsT", [P, GH, T])
        gaT = sb("gaT", [P, KD, T])
        gbT = sb("gbT", [P, KD, T])
        oT = sb("oT", [P, GROUP, T])
        b1T = sb("b1T", [P, EXPERTS, 2, KF])
        b2r = sb("b2r", [EXPERTS, D])
        w_glow = sb("w_glow", [P, KD, RANK])
        w_rt = sb("w_rt", [P, KD, EXPERTS])
        b_rt = sb("b_rt", [P, EXPERTS])
        wgk = sb("wgk", [RANK, GH * GDK])
        sinkc = sb("sinkc", [P, HEADS])
        sink_s = sb("sink_s", [P, KVH, GROUP])
        sinkr = sb("sinkr", [P, 3, 4])
        cols = sb("cols", [P, 21])
        kTok = sb("kTok", [P, 2, P])
        small = sb("small", [P, 64])
        dec = sb("dec", [P, PAIRS, NCH + NSEQ])
        sel = sb("sel", [P, 3, EXPERTS])
        gates = sb("gates", [P, 3, EXPERTS + 2])
        place = sb("place", [P, 3, EXPERTS + 2])
        most = sb("most", [1, 1], I32)

        def const(name, rows_=P):
            a, w = CONST_AT[name]
            return cst[0:rows_, a:a + w]

        ident = const("ident")
        late = ring[:, 4:6, :].rearrange("p a b -> p (a b)")
        ck = late[:, 0:1024].rearrange("p (b c) -> p b c", b=NSEQ)
        cv = late[:, 1024:2048].rearrange("p (b c) -> p b c", b=NSEQ)
        ckT = late[:, 2048:3072].rearrange("p (b c) -> p b c", b=NSEQ)
        S_at = late[:, 3072:4096]
        low = ring[:, 0:4, :].rearrange("p a b -> p (a b)")
        PT_ = PAIRS * T
        zb, lsp, B, D1, D2, q_in, k_in, q_out, k_out = (
            low[:, i * PT_:(i + 1) * PT_].rearrange("p (j t) -> p j t", j=PAIRS) for i in range(9))
        S_all = low[:, 9 * PT_:9 * PT_ + (NCH + 1) * 256].rearrange("p (c j v) -> p c j v", j=PAIRS, v=GDV)
        q_pair = low[:, 3 * PT_:5 * PT_].rearrange("p (a j t) -> p a j t", a=2, j=PAIRS)
        glT = low[0:RANK, 3 * PT_:3 * PT_ + T]
        AT_p = low[:, 0:1024].rearrange("p (h t j s) -> p h t j s", h=2, t=2, j=PAIRS)
        AT_s = low[:, 1024:1280].rearrange("p (h j s) -> p h j s", h=2, j=PAIRS)
        xn = region2[:, :].rearrange("p (t c) -> p t c", t=3)
        kM = region2[:, 0:1024].rearrange("p (c k) -> p c k", c=CPT)
        kMs = region2[:, 1024:3072].rearrange("p (c k) -> p c k", c=NSEQ)
        obT = region2[:, 1024:1024 + GH * T].rearrange("p (h t) -> p h t", h=GH)
        scratch = acc[:, :, :].rearrange("p t c -> p (t c)")
        raw = scratch[:, 0:640].rearrange("p (b t) -> p b t", b=2)
        squares = scratch[:, 640:1280].rearrange("p (b t) -> p b t", b=2)
        rstd_qk = scratch[:, 1280:1920].rearrange("p (b t) -> p b t", b=2)
        S0 = scratch[:, 0:2048].rearrange("p (b j v) -> p b j v", b=NSEQ, j=PAIRS)
        b1r = gbT[0:EXPERTS, :, :].rearrange("p a b -> p (a b)")[:, 0:2 * FF]
        qT = region_q[:, 0:1024].rearrange("p (j t) -> p j t", j=4)
        qS = region_q[:, 1024:1280].rearrange("p (b j t) -> p b j t", b=NSEQ, j=4)
        pT = region_q[:, 1280:2304].rearrange("p (k h q) -> p k h q", k=2, h=4)
        S_new = region_q[:, 0:2048].rearrange("p (b j v) -> p b j v", b=NSEQ, j=PAIRS)
        norm1_row, rows = oT[0:8, 0, 0:P], oT[0:13, 1, 0:P]
        squares_o = xnT[:, 0:4, :]
        rstd_o = xnT[:, 4:8, :]
        hnT = gaT
        moe = gbT[:, :, :].rearrange("p a b -> p (a b)")
        hn = region2[:, :].rearrange("p (t c) -> p t c", t=3)
        xeT = moe[:, 0:1024].rearrange("p (k s) -> p k s", k=KD)
        u_sb = moe[:, 1024:2048].rearrange("p (q c) -> p q c", q=2)
        moe2 = xnT[:, :, :].rearrange("p a b -> p (a b)")
        y_sb = moe2[:, 0:1024].rearrange("p (s c) -> p s c", s=2)
        hT = moe2[:, 1024:2048].rearrange("p (s f t) -> p s f t", s=2, f=KF)
        glu = moe2[:, 2048:2560].rearrange("p (f t) -> p f t", f=KF)
        moe3 = rbT[:, :, :].rearrange("p a b -> p (a b)")
        lin = moe3[:, 0:512].rearrange("p (f t) -> p f t", f=KF)
        sig = moe3[:, 512:1024].rearrange("p (f t) -> p f t", f=KF)
        pick = rsT[:, :, :].rearrange("p a b -> p (a b)")[:, 0:384].rearrange("p (t s) -> p t s", t=3)
        moe4 = oT[:, :, :].rearrange("p a b -> p (a b)")
        gpick = moe4[:, 0:768].rearrange("p (t s c) -> p t s c", t=3, s=2)
        gateT = moe4[0:EXPERTS, 768:768 + T]
        gpickT = rsT[:, :, :].rearrange("p a b -> p (a b)")[:, 384:1152].rearrange("p (s t) -> p s t", s=2)
        rt = qbT[:, :, :].rearrange("p a b -> p (a b)")
        lg = [rt[:, 32 * t:32 * t + 32] for t in range(3)]
        top8 = [rt[:, 96 + 8 * t:104 + 8 * t] for t in range(3)]
        idxf = [rt[:, 120 + 4 * t:124 + 4 * t] for t in range(3)]
        top_e = [rt[:, 132 + 4 * t:136 + 4 * t] for t in range(3)]
        onehot_g = [rt[:, 144 + 128 * t:272 + 128 * t].rearrange("p (k e) -> p k e", k=TOPK) for t in range(3)]
        onehot = [kbT[:, :, :].rearrange("p a b -> p (a b)")[:, 128 * t:128 * t + 128].rearrange("p (k e) -> p k e", k=TOPK)
                  for t in range(3)]
        top_neg, top_sum, top_inv = ([small[:, a + t:a + t + 1] for t in range(3)] for a in (0, 3, 6))
        idx8 = sb("idx8", [P, 3, 8], U32)

        ps = ctx.enter_context(nc.psum_tensor("ps", [P, 8, 512], F32))
        NB, XB, YB, VB_, WB = 3, 4, 5, 6, 7

        x_in = [sem(f"x_in{t}") for t in range(3)]
        ident_in, consts_in, rows_in, small_in, cache_in = (sem(n) for n in (
            "ident_in", "consts_in", "rows_in", "small_in", "cache_in"))
        b1_in, norm1_in = sem("b1_in"), sem("norm1_in")
        unit_in = [sem(f"unit_in{m}") for m in range(NU)]
        wa_in, wb_in, wo_in, s0_in = (sem(n) for n in ("wa_in", "wb_in", "wo_in", "s0_in"))
        x_again = [sem(f"x_again{t}") for t in range(3)]
        ss_ready, rstd_base, rstd_ready, xn_ready = (sem(n) for n in ("ss_ready", "rstd_base", "rstd_ready", "xn_ready"))
        xT_ready, xnT_ready = sem("xT_ready"), sem("xnT_ready")
        pj_ready, pj_freed = sem("pj_ready"), sem("pj_freed")
        sq_ready, var_ready, qk_rstd, qk_done = (sem(n) for n in ("sq_ready", "var_ready", "qk_rstd", "qk_done"))
        n_ready, n_freed = sem("n_ready"), sem("n_freed")
        xy_ready, xy_freed = sem("xy_ready"), sem("xy_freed")
        vw_ready, vw_freed = sem("vw_ready"), sem("vw_freed")
        gates_ready = sem("gates_ready")
        lsp_ready, decay_ready, exps_ready, gla_ops = (sem(n) for n in ("lsp_ready", "decay_ready", "exps_ready", "gla_ops"))
        max_ready, exp_done, p_ready = sem("max_ready"), sem("exp_done"), sem("p_ready")
        pads_ready, sqo_ready, varo_ready, rstdo_ready, ob_done = (sem(n) for n in (
            "pads_ready", "sqo_ready", "varo_ready", "rstdo_ready", "ob_done"))
        merged_ready, mg_ready, mg_freed = (sem(n) for n in ("merged_ready", "mg_ready", "mg_freed"))
        h_psum, h_ready, ss2_ready, base2_ready, rstd2_ready, hn_ready, hnT_psum, hnT_ready, lg_psum = (sem(n) for n in (
            "h_psum", "h_ready", "ss2_ready", "base2_ready", "rstd2_ready", "hn_ready", "hnT_psum", "hnT_ready", "lg_psum"))
        top_ready, gexp_ready, route_ready, pos_psum, gT_copied, sel_ready, gT_psum = (sem(n) for n in (
            "top_ready", "gexp_ready", "route_ready", "pos_psum", "gT_copied", "sel_ready", "gT_psum"))
        lgt_freed = sem("lgt_freed")
        act_steps, dve_steps = sem("act_steps"), sem("dve_steps")
        states_out, y_out = sem("states_out"), sem("y_out")
        stores, count_ready, slots_moved = sem("stores"), sem("count_ready"), sem("slots_moved")
        w1_in = [sem(f"w1_in{k}") for k in range(KD)]
        w1_early = [sem(f"w1_early{k}") for k in range(EARLY)]
        w2_in = [sem(f"w2_in{j}") for j in range(4)]
        w1_used, w2_used = sem("w1_used"), sem("w2_used")
        pick_ready, gpick_ready, gather_done, xe_ready, gpT_done, gpT_copied = (sem(n) for n in (
            "pick_ready", "gpick_ready", "gather_done", "xe_ready", "gpT_done", "gpT_copied"))
        u_copied, ut_done, glu_biased, glu_ready, lin_biased, lin_ready, sig_ready, prod_ready, h_act = (sem(n) for n in (
            "u_copied", "ut_done", "glu_biased", "glu_ready", "lin_biased", "lin_ready", "sig_ready", "prod_ready", "h_act"))
        y_copied, comb_done, comb_added = (sem(n) for n in ("y_copied", "comb_done", "comb_added"))

        def slot_of(m):
            return FIRST_SLOT + m % STREAM_SLOTS

        def unit(m):
            return ring[:, slot_of(m), :].rearrange("p (k c) -> p k c", k=KD)

        wa_sb = ring[:, 6:8, :].rearrange("p a b -> p (a b)").rearrange("p (k c) -> p k c", k=4)
        wb_sb = ring[:, 4:6, :].rearrange("p a b -> p (a b)").rearrange("p (k c) -> p k c", k=4)
        wo_sb = ring[:, 8:12, :].rearrange("p a b -> p (a b)").rearrange("p (k c) -> p k c", k=KD)
        w1v = w1.rearrange("l e (k p) c -> (l e) k p c", p=P)
        w2v = w2.rearrange("l e (j f p) c -> (l e) j p f c", f=2, p=P)

        def x_tile(t):
            return x_sample.rearrange("b t c -> (b t) c") if t == 2 else x_prompt[0, t * P:(t + 1) * P, :]

        def order_of(f):
            return f // 4 * 4 + f % 2 * 2 + f // 2 % 2

        block = ctx.enter_context(nc.Block())

        @block.sync
        def _(sp):
            for t, (_, r) in enumerate(TILES):
                sp.dma_start(acc[0:r, t, :], x_tile(t)).then_inc(x_in[t], 16)
                if t == 0:
                    sp.dma_start(cst[:, 0:2 * P], consts[:, 0:2 * P]).then_inc(ident_in, 16)
            for m in range(2):
                for j in range(2):
                    for g in range(KVH):
                        h = GROUP * g + 2 * m + j
                        sp.dma_start(unit(m)[:, :, P * j + HD * g:P * j + HD * g + HD],
                                     w_in[0, :, h * HD:(h + 1) * HD].rearrange("(k p) c -> p k c", p=P)
                                     ).then_inc(unit_in[m], 16)

            def load_unit(m):
                c = W_UNITS[m - 2]
                sp.dma_start(unit(m), w_in[0, :, c:c + UNIT].rearrange("(k p) c -> p k c", p=P)
                             ).then_inc(unit_in[m], 16)

            for m in range(2, STREAM_SLOTS):
                load_unit(m)
                if m == 2:
                    sp.dma_start(cst[:, 2 * P:NCONST], consts[:, 2 * P:NCONST]).then_inc(consts_in, 16)
            for m in range(STREAM_SLOTS, NU):
                sp.wait_ge(pj_ready, unit_done(m - STREAM_SLOTS))
                load_unit(m)
                if m == STREAM_SLOTS + 2:
                    sp.wait_ge(qk_done, 5)
                    sp.dma_start(S0.rearrange("p b j v -> p (b j) v"),
                                 state_gla[0].rearrange("b (j a) k v -> (a k) (b j) v", a=2)).then_inc(s0_in, 16)
            sp.wait_ge(pj_ready, unit_done(13))
            for g in range(KVH):
                sp.dma_start(wa_sb[HD * g:HD * g + HD, :, :],
                             w_a[0, 256 * g:256 * g + 256, :].rearrange("(j d) c -> d j c", d=HD)).then_inc(wa_in, 16)
            sp.wait_ge(n_ready, use(N_USES, "attend4"))
            sp.dma_start(wb_sb, w_b[0].rearrange("(h v) c -> v h c", v=GDV)).then_inc(wb_in, 16)
            sp.wait_ge(pj_ready, len(TILE_ORDER))
            sp.dma_start(wo_sb, w_o[0].rearrange("(k p) c -> p k c", p=P)).then_inc(wo_in, 16)
            sp.wait_ge(vw_ready, use(VW_USES, "gla_s"))
            sp.wait_ge(xy_freed, use(XY_USES, "state3"))
            for t, (_, r) in enumerate(TILES):
                sp.dma_start(acc[0:r, t, :], x_tile(t)).then_inc(x_again[t], 16)

            def load_w1(n, e, k):
                sp.dma_start(ring[:, k, :], w1v[e, k]).then_inc(w1_in[k], 16)

            def load_w2(n, e, j):
                sp.dma_start(ring[:, 8 + j, :].rearrange("p (f c) -> p f c", f=2), w2v[e, j]).then_inc(w2_in[j], 16)

            def next_w1(n, e, first_k=0):
                for k in range(first_k, KD):
                    sp.wait_ge(w1_used, (n - 1) * KD + k + 1)
                    load_w1(n, e, k)

            def next_w2(n, e):
                for j in range(4):
                    sp.wait_ge(w2_used, (n - 1) * 4 + j + 1)
                    load_w2(n, e, j)

            def last_loads(base):
                next_w2(base + EXPERTS - 2, EXPERTS - 2)
                next_w1(base + EXPERTS - 1, EXPERTS - 1)
                next_w2(base + EXPERTS - 1, EXPERTS - 1)

            sp.wait_ge(states_out, 32)
            for k in range(EARLY):
                sp.dma_start(early[:, k, :], w1v[0, k]).then_inc(w1_early[k], 16)
            for k in range(EARLY, 4):
                load_w1(0, 0, k)
            sp.wait_ge(merged_ready, KD)
            for k in range(4, KD):
                load_w1(0, 0, k)
            sp.wait_ge(h_psum, 3)
            for j in range(4):
                load_w2(0, 0, j)
            for k in range(EARLY):
                load_w1(1, 1, k)
            next_w1(1, 1, EARLY)
            with sp.Fori(2, EXPERTS - 1) as n:
                next_w1(n, n)
                next_w2(n - 1, n - 1)
            last_loads(0)
            def store_tile(t):
                r = TILES[t][1]
                dst = y_sample.rearrange("b t c -> (b t) c") if t == 2 else y_prompt[0, t * P:(t + 1) * P, :]
                sp.dma_start(dst, acc[0:r, t, :]).then_inc(y_out, 16)

            sp.wait_ge(count_ready, 1)
            busiest = sp.value_load(most[0:1, 0:1], min_val=0, max_val=T)
            HALF = EXPERTS // 2
            with sp.If(busiest > SLOTS):
                with sp.Fori(1, PASSES) as b:
                    next_w1(EXPERTS * b, 0)
                    with sp.Fori(1, EXPERTS - 1) as n:
                        next_w1(EXPERTS * b + n, n)
                        next_w2(EXPERTS * b + n - 1, n - 1)
                    last_loads(EXPERTS * b)
                sp.wait_ge(comb_added, 3 * (HALF * PASSES + 1))
                sp.nop()
            for t in range(3):
                sp.wait_ge(comb_added, 3 * HALF + t + 1)
                store_tile(t)
            sp.wait_ge(stores, 16 * 20)
            sp.wait_ge(y_out, 16 * 3)

        @block.gpsimd
        def _(pool):
            pool.dma_start(rows[0:8, :], norm2.rearrange("l (k p) -> (l k) p", p=P)).then_inc(rows_in, 16)
            for at, vector in ((10, q_norm), (11, k_norm)):
                pool.dma_start(rows[at:at + 1, :].rearrange("p (g d) -> p g d", g=KVH),
                               vector.unsqueeze(1).broadcast_to([1, KVH, HD])).then_inc(rows_in, 16)
            pool.dma_start(rows[8:10, :], b_gk.rearrange("l (k p) -> (l k) p", p=P)).then_inc(rows_in, 16)
            pool.dma_start(rows[12:13, :], gla_norm).then_inc(rows_in, 16)
            pool.memset(place[:, :, :], 0.0).then_inc(pads_ready, 1)
            pool.memset(gates[:, :, :], 0.0).then_inc(pads_ready, 1)
            pool.memset(sel[:, :, :], 0.0).then_inc(pads_ready, 1)
            pool.wait_ge(pads_ready, 3)
            pool.memset(vB[64:128, 2, :], 0.0).then_inc(pads_ready, 1)
            pool.wait_ge(unit_in[0], 64)
            pool.dma_start(b1r, b1[0]).then_inc(b1_in, 16)
            pool.dma_start(w_glow[:, :, :], w_in[0, :, C_GLOW:C_RB].rearrange("(k p) c -> p k c", p=P)).then_inc(small_in, 16)
            pool.dma_start(wgk[:, :], w_gk[0]).then_inc(small_in, 16)
            pool.dma_start(sinkc[:, :], sinks.partition_broadcast(P).rearrange("p a h -> p (a h)")).then_inc(small_in, 16)
            pool.dma_start(ck, cache_k[0].rearrange("b w g d -> w b (g d)")).then_inc(cache_in, 16)
            pool.dma_start(cv, cache_v[0].rearrange("b w g d -> w b (g d)")).then_inc(cache_in, 16)
            pool.dma_start(w_rt[:, :, :], w_router[0].rearrange("(k p) e -> p k e", p=P)).then_inc(small_in, 16)
            pool.dma_start(b_rt[:, :], b_router.partition_broadcast(P).rearrange("p a h -> p (a h)")).then_inc(small_in, 16)
            pool.dma_start(b2r[:, :], b2[0]).then_inc(small_in, 16)
            for dst, src in ((k_sample, cache_k), (v_sample, cache_v)):
                pool.dma_start(dst[0, :, 0:P - TSEQ].rearrange("b w g d -> b w (g d)"),
                               src[0, :, TSEQ:P].rearrange("b w g d -> b w (g d)")).then_inc(stores, 16)
            pool.wait_ge(pj_freed, 8)
            pool.dma_start(v_prompt[0, 0].rearrange("w g d -> w (g d)"), vA[:, 1, :]).then_inc(stores, 16)
            for b in range(NSEQ):
                pool.dma_start(v_sample[0, b, P - TSEQ:P].rearrange("w g d -> w (g d)"),
                               vA[TSEQ * b:TSEQ * b + TSEQ, 2, :]).then_inc(stores, 16)
            pool.wait_ge(n_freed, use(N_USES, "keys"))
            pool.dma_start(k_prompt[0, 0].rearrange("w g d -> w (g d)"), kTok[:, 0, :]).then_inc(stores, 16)
            for b in range(NSEQ):
                pool.dma_start(k_sample[0, b, P - TSEQ:P].rearrange("w g d -> w (g d)"),
                               kTok[TSEQ * b:TSEQ * b + TSEQ, 1, :]).then_inc(stores, 16)
            pool.wait_ge(xy_freed, use(XY_USES, "state3"))
            pool.dma_start(s_prompt[0, 0].rearrange("(j a) k v -> (a k) j v", a=2), S_all[:, NCH, :, :]).then_inc(states_out, 16)
            pool.dma_start(s_sample[0].rearrange("b (j a) k v -> (a k) (b j) v", a=2),
                           S_new.rearrange("p b j v -> p (b j) v")).then_inc(states_out, 16)

        @block.tensor
        def _(pe):
            def take(uses, freed, name):
                if use(uses, name) > 1:
                    pe.wait_ge(freed, use(uses, name) - 1)

            pe.wait_ge(ident_in, 16)
            pe.wait_ge(norm1_in, 16)
            pe.transpose(ps[:, NB, 0:8], norm1_row[:, :], ident[0:8, 0:8]).then_inc(n_ready, 1)
            for t, (_, r) in enumerate(TILES):
                pe.wait_ge(xn_ready, t + 1)
                for half in range(2):
                    u = 2 * t + half
                    if u >= 4:
                        pe.wait_ge(xnT_ready, u - 3)
                    for k in range(4):
                        mm = pe.transpose(ps[:, XB + u % 4, P * k:P * k + r],
                                          xn[0:r, t, P * (4 * half + k):P * (4 * half + k) + P], ident[0:r, 0:r])
                    mm.then_inc(xT_ready, 1)

            pe.wait_ge(xnT_ready, 6)

            def vectors_to_columns():
                pe.wait_ge(rows_in, 16 * 5)
                take(N_USES, n_freed, "vectors")
                pe.transpose(ps[:, NB, 0:13], rows[:, :], ident[0:13, 0:13]).then_inc(n_ready, 1)

            def b1_to_columns():
                pe.wait_ge(b1_in, 16)
                take(N_USES, n_freed, "b1")
                for gl in range(2):
                    for f in range(KF):
                        c = 256 * f + gl
                        mm = pe.transpose(ps[:, NB, (gl * KF + order_of(f)) * EXPERTS:(gl * KF + order_of(f) + 1) * EXPERTS],
                                          b1r[:, c:c + 255:2], ident[0:EXPERTS, 0:EXPERTS])
                mm.then_inc(n_ready, 1)

            unit_at = [0]

            def need_unit(m):
                if m >= unit_at[0]:
                    pe.wait_ge(unit_in[m], 64 if m < 2 else 16)
                    unit_at[0] = m + 1

            def project(n):
                kind, j = TILE_ORDER[n]
                bank = n % 3
                if n >= 3:
                    pe.wait_ge(pj_freed, n - 2)
                if kind in ("va", "vb"):
                    t0, r = TILES[j]
                    if kind == "va":
                        for k in range(KD):
                            mm = pe.matmul(ps[0:r, bank, 0:P], xnT[:, k, t0:t0 + r], unit(2)[:, k, P:2 * P],
                                           start=(k == 0), stop=(k == KD - 1))
                    else:
                        for c in range(2):
                            need_unit(5 + c)
                        if j < 2:
                            for c in range(2):
                                for k in range(KD):
                                    mm = pe.matmul(ps[:, bank, UNIT * c:UNIT * c + UNIT], xnT[:, k, t0:t0 + r],
                                                   unit(5 + c)[:, k, :], start=(k == 0), stop=(k == KD - 1))
                        else:
                            for k in range(KD):
                                for c in range(2):
                                    mm = pe.matmul(ps[64 * c:64 * c + 64, bank, 0:UNIT], xnT[:, k, t0:t0 + r],
                                                   unit(5 + c)[:, k, :], start=(k == 0), stop=(k == KD - 1))
                    mm.then_inc(pj_ready, 1)
                    return
                if kind == "glow":
                    pe.wait_ge(small_in, 16 * 6)
                    pe.wait_ge(consts_in, 16)
                    for k in range(KD):
                        mm = pe.matmul(ps[0:RANK, bank, 0:T], w_glow[:, k, :], xnT[:, k, :],
                                       start=(k == 0), stop=(k == KD - 1))
                    mm.then_inc(pj_ready, 1)
                    return
                m = {"q": 0, "k": 2, "qb": 3, "kb": 4, "rb": 7, "ga": 9, "gb": 13}[kind] + j // 2
                need_unit(m)
                c = P * (j % 2)
                for k in range(KD):
                    mm = pe.matmul(ps[:, bank, 0:T], unit(m)[:, k, c:c + P], xnT[:, k, :],
                                   start=(k == 0), stop=(k == KD - 1))
                mm.then_inc(pj_ready, 1)

            def norm_sum(j):
                take(N_USES, n_freed, f"norm{j}")
                pe.wait_ge(sq_ready, j + 1)
                pe.matmul(ps[:, NB, 0:T], const("head_mean"), squares[:, j % 2, :], start=True, stop=True
                          ).then_inc(n_ready, 1)

            def gate_logits():
                take(XY_USES, xy_freed, "z")
                pe.wait_ge(pj_freed, tiles_done("glow", 0))
                for j in range(PAIRS):
                    mm = pe.matmul(ps[:, XB + j, 0:T], wgk[:, P * j:P * j + P], glT[:, :], start=True, stop=True)
                mm.then_inc(xy_ready, 1)

            def cache_keys():
                take(VW_USES, vw_freed, "cache")
                pe.wait_ge(cache_in, 32)
                for b in range(NSEQ):
                    mm = pe.transpose(ps[:, VB_ + b // 4, P * (b % 4):P * (b % 4) + P], ck[:, b, :], ident)
                mm.then_inc(vw_ready, 1)

            def new_keys():
                take(N_USES, n_freed, "keys")
                pe.wait_ge(qk_done, 5)
                pe.transpose(ps[:, NB, 0:P], kT[:, P:2 * P], ident)
                pe.transpose(ps[0:64, NB, P:2 * P], kT[:, PROMPT:T], ident).then_inc(n_ready, 1)

            def scores(s):
                take(XY_USES, xy_freed, f"scores{s}")
                if s < 4:
                    n, i = divmod(s, 2)
                    first = 0 if n else P
                    w = 256 if n else P
                    for jj in range(2):
                        for g in range(KVH):
                            mm = pe.matmul(ps[:, XB + g, 256 * jj:256 * jj + w],
                                           qT[HD * g:HD * g + HD, 2 * i + jj, P * n:P * n + P],
                                           kT[HD * g:HD * g + HD, P * n - P + first:P * n + P], start=True, stop=True)
                else:
                    pe.wait_ge(vw_freed, 1)
                    for b in range(NSEQ):
                        hf, q = divmod(b, 4)
                        for g in range(KVH):
                            lhs = qS[HD * g:HD * g + HD, b, :, :].rearrange("p j t -> p (j t)")
                            out = ps[32 * q:32 * q + 32, XB + g, 192 * hf:192 * hf + 192]
                            pe.matmul(out[:, 0:P], lhs, ckT[HD * g:HD * g + HD, b, :], start=True, stop=True)
                            mm = pe.matmul(out[:, P:192], lhs, kT[HD * g:HD * g + HD, PROMPT:T], start=True, stop=True)
                mm.then_inc(xy_ready, 1)

            S_p = [S_at.rearrange("p (h c) -> p h c", h=4), S_at[:, 0:768].rearrange("p (h c) -> p h c", h=4)]

            def turn_probs(s):
                take(VW_USES, vw_freed, f"probs{s}")
                pe.wait_ge(p_ready, s + 1)
                for h in range(4):
                    if s < 4:
                        if s >= 2:
                            pe.transpose(ps[:, VB_, P * h:P * h + P], S_p[0][:, h, 0:P], ident)
                        mm = pe.transpose(ps[:, WB, P * h:P * h + P], S_p[0][:, h, P:2 * P], ident)
                    else:
                        pe.transpose(ps[:, VB_, P * h:P * h + P], S_p[1][:, h, 0:P], ident)
                        mm = pe.transpose(ps[0:64, WB, P * h:P * h + P], S_p[1][:, h, P:192], ident)
                mm.then_inc(vw_ready, 1)

            def attend(s):
                take(N_USES, n_freed, f"attend{s}")
                pe.wait_ge(vw_freed, use(VW_USES, f"probs{s}"))
                for g in range(KVH):
                    out = ps[HD * g:HD * g + HD, NB, :]
                    if s < 4:
                        blocks = [1] if s < 2 else [0, 1]
                        for kb in blocks:
                            mm = pe.matmul(out[:, 0:256], vA[:, s // 2 - 1 + kb, HD * g:HD * g + HD],
                                           pT[:, kb, 2 * g:2 * g + 2, :].rearrange("p h q -> p (h q)"),
                                           start=(kb == blocks[0]), stop=(kb == 1))
                    else:
                        for hf in range(2):
                            pe.matmul(out[:, P * hf:P * hf + P], vA[0:64, 2, HD * g:HD * g + HD], pT[0:64, 1, 2 * g + hf, :],
                                      start=True, stop=False, skip_group_check=True)
                            for q in range(4):
                                mm = pe.matmul(out[:, P * hf + 32 * q:P * hf + 32 * q + 32],
                                               cv[:, 4 * hf + q, HD * g:HD * g + HD],
                                               pT[:, 0, 2 * g + hf, 32 * q:32 * q + 32],
                                               start=False, stop=(q == 3), skip_group_check=True)
                mm.then_inc(n_ready, 1)

            def decays(name, tiles):
                take(XY_USES, xy_freed, name)
                pe.wait_ge(gla_ops, 1)
                for t in tiles:
                    t0, r = TILES[t]
                    for j in range(PAIRS):
                        for a in range(2):
                            at = P * (2 * t + j) if t < 2 else 64 * j
                            mm = pe.matmul(ps[0:r, XB + a, at:at + r], k_in[64 * a:64 * a + 64, j, t0:t0 + r],
                                           q_in[64 * a:64 * a + 64, j, t0:t0 + r], start=True, stop=True)
                mm.then_inc(xy_ready, 1)

            def turn_keys(t):
                take(N_USES, n_freed, f"gkeys{t}")
                pe.wait_ge(gla_ops, 1)
                t0, r = TILES[t]
                for j in range(PAIRS):
                    mm = pe.transpose(ps[0:r, NB, P * j:P * j + P], k_out[:, j, t0:t0 + r], ident)
                mm.then_inc(n_ready, 1)

            def state_steps(which):
                take(XY_USES, xy_freed, f"state{which}")
                pe.wait_ge(n_freed, use(N_USES, f"gkeys{min(which, 2)}"))
                t = min(which, 2)
                r = TILES[t][1]
                for c in range(4):
                    keys = kM[:, c, :] if which < 2 else kMs[0:64, 4 * (which - 2) + c, :]
                    for j in range(PAIRS):
                        for a in range(2):
                            o = 256 * (c % 2) + P * j
                            mm = pe.matmul(ps[64 * a:64 * a + 64, XB + c // 2, o:o + P],
                                           keys[:, P * j + 64 * a:P * j + 64 * a + 64],
                                           vB[0:r, t, P * (2 * j + a):P * (2 * j + a) + P], start=True, stop=True)
                mm.then_inc(xy_ready, 1)

            def gla_out(sample):
                take(VW_USES, vw_freed, "gla_s" if sample else "gla_p")
                pe.wait_ge(xy_freed, use(XY_USES, "state1"))
                if sample:
                    pe.wait_ge(pads_ready, 4)
                    pe.wait_ge(s0_in, 16)
                for j in range(PAIRS):
                    bank = ps[:, VB_ + j, 0:2 * (T - PROMPT if sample else PROMPT)].rearrange("p (a q) -> p a q", a=2)
                    if sample:
                        for a in range(2):
                            pe.matmul(bank[:, a, :], vB[:, 2, P * (2 * j + a):P * (2 * j + a) + P], AT_s[:, a, j, :],
                                      start=(a == 0), stop=False, skip_group_check=True)
                        for b in range(NSEQ):
                            s0 = TSEQ * b
                            mm = pe.matmul(bank[:, :, s0:s0 + TSEQ], S0[:, b, j, :],
                                           q_pair[:, :, j, PROMPT + s0:PROMPT + s0 + TSEQ],
                                           start=False, stop=(b == NSEQ - 1), skip_group_check=True)
                    else:
                        for a in range(2):
                            for t in range(2):
                                pe.matmul(bank[:, a, P * t:P * t + P], vB[:, t, P * (2 * j + a):P * (2 * j + a) + P],
                                          AT_p[:, a, t, j, :], start=(a == t == 0), stop=False, skip_group_check=True)
                        for c in range(1, NCH):
                            s0 = CHUNK * c
                            mm = pe.matmul(bank[:, :, s0:s0 + CHUNK], S_all[:, c, j, :], q_pair[:, :, j, s0:s0 + CHUNK],
                                           start=False, stop=(c == NCH - 1), skip_group_check=True)
                mm.then_inc(vw_ready, 1)

            def dv_sum(h):
                take(N_USES, n_freed, f"dv{h}")
                pe.wait_ge(sqo_ready, 1)
                pe.matmul(ps[:, NB, 0:T], const("dv_mean"), squares_o[:, h, :], start=True, stop=True
                          ).then_inc(n_ready, 1)

            for n in range(FIRST_RB):
                project(n)
                if n == 1:
                    vectors_to_columns()
                if 1 <= n <= 5:
                    norm_sum(n - 1)
                if n == 6:
                    b1_to_columns()
            between = {
                0: [gate_logits, cache_keys],
                1: [new_keys, lambda: scores(0)],
                4: [lambda: turn_probs(0), lambda: scores(1)],
                5: [lambda: attend(0)],
                6: [lambda: turn_probs(1), lambda: scores(2)],
                7: [lambda: attend(1)],
                8: [lambda: turn_probs(2), lambda: scores(3)],
                9: [lambda: attend(2)],
                10: [lambda: turn_probs(3), lambda: scores(4)],
                11: [lambda: attend(3)],
                12: [lambda: turn_probs(4), lambda: decays("decays_p", [0, 1])],
                13: [lambda: attend(4), lambda: decays("decays_s", [2])],
                14: [lambda: turn_keys(0)],
                15: [lambda: state_steps(0), lambda: turn_keys(1)],
                16: [lambda: state_steps(1), lambda: turn_keys(2)],
                17: [lambda: state_steps(2), lambda: gla_out(False)],
                18: [lambda: state_steps(3)],
                19: [lambda: gla_out(True)],
            }
            for s in range(20):
                project(FIRST_RB + s)
                for step in between.get(s, ()):
                    step()

            def branch(w_sb, operand, m, u):
                if u < 3:
                    pe.wait_ge(pj_freed, len(TILE_ORDER))
                else:
                    pe.wait_ge(mg_freed, u - 2)
                for k in range(4):
                    mm = pe.matmul(ps[:, u % 3, 0:T], w_sb[:, k, P * m:P * m + P], operand[:, k, :],
                                   start=(k == 0), stop=(k == 3))
                mm.then_inc(mg_ready, 1)

            pe.wait_ge(wa_in, 32)
            pe.wait_ge(n_freed, use(N_USES, "attend4"))
            for m in range(KD):
                branch(wa_sb, oT, m, m)
                if 1 <= m <= GH:
                    dv_sum(m - 1)
            pe.wait_ge(wb_in, 16)
            pe.wait_ge(ob_done, GH)
            for m in range(KD):
                branch(wb_sb, obT, m, KD + m)
            TURN_BANK = (0, VB_, 0)
            def project_h(t):
                t0, r = TILES[t]
                if t == 0:
                    pe.wait_ge(xy_freed, len(XY_USES))
                if t == 1:
                    pe.wait_ge(vw_freed, len(VW_USES))
                if t == 2:
                    pe.wait_ge(h_ready, 1)
                if t < 2:
                    for c in range(2):
                        for k in range(KD):
                            mm = pe.matmul(ps[:, (XB, VB_)[t] + c, :], xnT[:, k, t0:t0 + r],
                                           wo_sb[:, k, 512 * c:512 * c + 512], start=(k == 0), stop=(k == KD - 1))
                else:
                    for k in range(KD):
                        for c in range(2):
                            mm = pe.matmul(ps[64 * c:64 * c + 64, XB, :], xnT[:, k, t0:t0 + r],
                                           wo_sb[:, k, 512 * c:512 * c + 512], start=(k == 0), stop=(k == KD - 1))
                mm.then_inc(h_psum, 1)

            def turn_h(t):
                t0, r = TILES[t]
                pe.wait_ge(h_ready, t + 1)
                if t == 0:
                    pe.wait_ge(mg_freed, 2 * KD)
                if t == 2:
                    pe.wait_ge(hnT_ready, 1)
                for k in range(KD):
                    mm = pe.transpose(ps[:, TURN_BANK[t] + k // 4, P * (k % 4):P * (k % 4) + r], acc[0:r, t, P * k:P * k + P],
                                      ident[0:r, 0:r])
                mm.then_inc(hnT_psum, 1)

            def logits(t):
                t0, r = TILES[t]
                pe.wait_ge(hnT_ready, t + 1)
                if t:
                    pe.wait_ge(lgt_freed, t)
                for k in range(KD):
                    mm = pe.matmul(ps[0:r, 2, 0:EXPERTS], hnT[:, k, t0:t0 + r], w_rt[:, k, :],
                                   start=(k == 0), stop=(k == KD - 1))
                mm.then_inc(lg_psum, 1)

            def places(t):
                r = TILES[t][1]
                pe.wait_ge(sel_ready, t + 1)
                for s in range(t + 1):
                    rr = TILES[s][1]
                    mm = pe.matmul(ps[0:r, NB, EXPERTS * t:EXPERTS * (t + 1)],
                                   (const("before") if s == t else const("ones"))[0:rr, 0:r], sel[0:rr, s, :],
                                   start=(s == 0), stop=(s == t))
                mm.then_inc(pos_psum, 1)

            pe.wait_ge(wo_in, 16)
            pe.wait_ge(merged_ready, KD)
            project_h(0)
            project_h(1)
            turn_h(0)
            project_h(2)
            turn_h(1)
            logits(0)
            turn_h(2)
            logits(1)
            logits(2)
            pe.wait_ge(pads_ready, 4)
            pe.wait_ge(n_freed, len(N_USES))
            for t in range(3):
                places(t)
            for t, (_, r) in enumerate(TILES):
                mm = pe.matmul(ps[0:1, NB, 96:128], const("ones")[0:r, 0:1], sel[0:r, t, :],
                               start=(t == 0), stop=(t == 2))
            mm.then_inc(pos_psum, 1)

            def turn_dense_gates():
                pe.wait_ge(route_ready, 1)
                pe.wait_ge(lgt_freed, 3)
                for t, (t0, r) in enumerate(TILES):
                    mm = pe.transpose(ps[0:EXPERTS, 6, t0:t0 + r], gates[0:r, t, 0:EXPERTS], ident[0:r, 0:r])
                mm.then_inc(gT_psum, 1)

            def gather(p, gates_copied, fresh=False):
                for half in range(2):
                    bank = 7 - half if fresh else 7
                    if half == 0:
                        pe.wait_ge(pick_ready, p + 1)
                        if gates_copied is not None:
                            pe.wait_ge(gpT_copied, gates_copied)
                    elif not fresh:
                        pe.wait_ge(xe_ready, 2 * p + 1)
                    for k in range(4):
                        for t, (_, r) in enumerate(TILES):
                            c = P * (4 * half + k)
                            mm = pe.matmul(ps[:, bank, P * k:P * k + P], hn[0:r, t, c:c + P], pick[0:r, t, :],
                                           start=(t == 0), stop=(t == 2))
                    mm.then_inc(gather_done, 1)

            def up(n, which, first=False):
                if not first:
                    pe.wait_ge(u_copied, n)
                for k in range(KD):
                    if which == 0 and k % 4 == 0:
                        pe.wait_ge(xe_ready, n + 1 + k // 4)
                    if first and k < EARLY:
                        pe.wait_ge(w1_early[k], 16)
                        tile = early[:, k, :]
                    else:
                        pe.wait_ge(w1_in[k], 16 * n + (0 if k < EARLY else 16))
                        tile = ring[:, k, :]
                    for q in range(4):
                        o = 64 * (q % 2)
                        mm = pe.matmul(ps[o:o + 64, q // 2, :], xeT[:, k, SLOTS * which:SLOTS * (which + 1)],
                                       tile[:, 512 * q:512 * q + 512], start=(k == 0), stop=(k == KD - 1))
                    mm.then_inc(w1_used, 1)

            def turn(n, first=False):
                pe.wait_ge(u_copied, n + 1)
                if not first:
                    pe.wait_ge(lin_biased, n)
                elif n == 0:
                    pe.wait_ge(count_ready, 1)
                for gl in range(2):
                    for q in range(2):
                        for r in range(2):
                            o = 256 * q + P * r
                            mm = pe.transpose(ps[:, 2 + gl, o:o + P], u_sb[:, q, 256 * r + gl:256 * r + gl + 255:2], ident)
                mm.then_inc(ut_done, 1)

            def down(n, which, first=False):
                pe.wait_ge(h_act, n + 1)
                if not first:
                    pe.wait_ge(y_copied, n)
                for f in range(KF):
                    if f % 2 == 0:
                        pe.wait_ge(w2_in[f // 2], 16 * n + 16)
                    for c in range(2):
                        mm = pe.matmul(ps[64 * c:64 * c + 64, 6, :], hT[:, which, order_of(f), :],
                                       ring[:, 8 + f // 2, D * (f % 2) + 512 * c:D * (f % 2) + 512 * c + 512],
                                       start=(f == 0), stop=(f == KF - 1))
                    if f % 2:
                        mm.then_inc(w2_used, 1)

            def turn_gates(p, last):
                for which in range(2):
                    if which == 0:
                        pe.wait_ge(gpick_ready, p + 1)
                        pe.wait_ge(xe_ready, 2 * p + (2 if last else 4))
                    else:
                        pe.wait_ge(gpT_copied, 2 * p + 1)
                    for t, (t0, r) in enumerate(TILES):
                        mm = pe.transpose(ps[:, 7, t0:t0 + r], gpick[0:r, t, which, :], ident[0:r, 0:r])
                    mm.then_inc(gpT_done, 1)

            def combine(c, t, biases=False, bank=XB):
                if bank == XB and not (biases and t == 0):
                    pe.wait_ge(comb_added, c)
                t0, r = TILES[t]
                for half in range(2):
                    if biases:
                        mm = pe.matmul(ps[0:r, bank + half, :], gateT[:, t0:t0 + r], b2r[:, 512 * half:512 * half + 512],
                                       start=True, stop=True)
                if not biases:
                    scatter(bank, t, (0, 1)).then_inc(comb_done, 1)
                else:
                    mm.then_inc(comb_done, 1)

            def scatter(bank, t, experts):
                t0 = TILES[t][0]
                for which in experts:
                    for half in range(2):
                        mm = pe.matmul(ps[:, bank + half, :], gpickT[64 * half:64 * half + 64, which, t0:t0 + P],
                                       y_sb[64 * half:64 * half + 64, which, :], start=(which == 0), stop=(which == 1))
                return mm

            def body(p, first=False, main=False):
                fresh = first and main
                if first:
                    gather(p, None if main else 2 * p, fresh)
                if first and not main:
                    pe.wait_ge(comb_added, 3 * p + 3)
                up(2 * p, 0, first=fresh)
                if not first:
                    down(2 * p - 1, 1)
                elif main:
                    turn_dense_gates()
                turn(2 * p, first=fresh)
                if not first:
                    pe.wait_ge(y_copied, 2 * p)
                    combine(3 * p, 0)
                elif main:
                    pe.wait_ge(gT_copied, 1)
                    combine(0, 0, biases=True)
                up(2 * p + 1, 1)
                if not first or main:
                    combine(3 * p + 1, 1, biases=first)
                    pe.wait_ge(lin_biased, 2 * p + 1)
                    combine(3 * p + 2, 2, biases=first, bank=2)
                down(2 * p, 0, first=fresh)
                gather(p + 1, None if fresh else 2 * p)
                turn_gates(p, False)
                pe.wait_ge(comb_added, 3 * p + 3)
                turn(2 * p + 1)

            def last_body(p):
                up(2 * p, 0)
                turn(2 * p)
                down(2 * p - 1, 1)
                pe.wait_ge(y_copied, 2 * p)
                banks = (XB, 0, 2)
                pe.wait_ge(u_copied, 2 * p + 1)
                combine(3 * p, 0)
                combine(3 * p + 1, 1, bank=0)
                pe.wait_ge(lin_biased, 2 * p + 1)
                combine(3 * p + 2, 2, bank=2)
                turn_gates(p, True)
                down(2 * p, 0)
                pe.wait_ge(comb_added, 3 * p + 3)
                up(2 * p + 1, 1)
                turn(2 * p + 1)
                pe.wait_ge(gpT_copied, 2 * p + 2)
                pe.wait_ge(y_copied, 2 * p + 1)
                pe.wait_ge(u_copied, 2 * p + 2)
                scatter(banks[0], 0, (0,))
                scatter(banks[1], 1, (0,))
                pe.wait_ge(lin_biased, 2 * p + 2)
                scatter(banks[2], 2, (0,))
                down(2 * p + 1, 1)
                pe.wait_ge(y_copied, 2 * p + 2)
                for t in range(3):
                    scatter(banks[t], t, (1,)).then_inc(comb_done, 1)

            HALF = EXPERTS // 2
            pe.wait_ge(hn_ready, 3)
            pe.wait_ge(h_ready, 3)
            body(0, first=True, main=True)
            with pe.Fori(1, HALF - 1) as i:
                body(i)
            last_body(HALF - 1)
            pe.wait_ge(count_ready, 1)
            busiest = pe.value_load(most[0:1, 0:1], min_val=0, max_val=T)
            with pe.If(busiest > SLOTS):
                with pe.Fori(1, PASSES) as b:
                    body(HALF * b, first=True)
                    with pe.Fori(1, HALF - 1) as i:
                        body(HALF * b + i)
                    last_body(HALF * b + HALF - 1)
                pe.nop()
            pe.nop()

        @block.scalar
        def _(act):
            steps = [0]

            def link(ins):
                steps[0] += 1
                ins.then_inc(act_steps, 1)
                act.wait_ge(act_steps, steps[0])

            act.dma_start(norm1_row[:, :], norm1.rearrange("l (k p) -> (l k) p", p=P)).then_inc(norm1_in, 16)
            for t, (_, r) in enumerate(TILES):
                act.wait_ge(x_in[t], 16)
                nc.scalar.activation(xn[0:r, t, :], acc[0:r, t, :], ACT.Square,
                                     accum_out=small[0:r, t:t + 1]).then_inc(ss_ready, 1)
            for t, (_, r) in enumerate(TILES):
                act.wait_ge(rstd_base, t + 1)
                nc.scalar.activation(small[0:r, 8 + t:9 + t], small[0:r, 4 + t:5 + t], ACT.Sqrt).then_inc(rstd_ready, 1)

            def evacuate(n):
                kind, j = TILE_ORDER[n]
                src = ps[:, n % 3, 0:T]
                act.wait_ge(pj_ready, n + 1)
                if kind in ("q", "k"):
                    b = n % 2
                    if n >= 2:
                        act.wait_ge(qk_done, n - 1)
                    else:
                        act.wait_ge(xn_ready, 3)
                    nc.scalar.activation(squares[:, b, :], src, ACT.Square).then_inc(sq_ready, 1)
                    nc.scalar.copy(raw[:, b, :], src).then_inc(pj_freed, 1)
                elif kind in ("va", "vb"):
                    r = TILES[j][1]
                    if kind == "va":
                        nc.scalar.copy(vA[0:r, j, :], ps[0:r, n % 3, 0:P]).then_inc(pj_freed, 1)
                    elif j < 2:
                        nc.scalar.copy(vB[:, j, :], ps[:, n % 3, :]).then_inc(pj_freed, 1)
                    else:
                        nc.scalar.copy(vB[0:64, j, 0:UNIT], ps[0:64, n % 3, 0:UNIT])
                        nc.scalar.copy(vB[0:64, j, UNIT:2 * UNIT], ps[64:128, n % 3, 0:UNIT]).then_inc(pj_freed, 1)
                elif kind == "qb":
                    nc.scalar.activation(qbT[:, j, :], src, ACT.Copy, scale=SCALE).then_inc(pj_freed, 1)
                elif kind == "kb":
                    nc.scalar.copy(kbT[:, j, :], src).then_inc(pj_freed, 1)
                elif kind == "glow":
                    nc.scalar.copy(glT[:, :], ps[0:RANK, n % 3, 0:T]).then_inc(pj_freed, 1)
                elif kind == "rb":
                    nc.scalar.copy(rbT[:, j, :], src).then_inc(pj_freed, 1)
                elif kind == "ga":
                    nc.scalar.copy(gaT[:, j, :], src).then_inc(pj_freed, 1)
                else:
                    nc.scalar.activation(gbT[:, j, :], src, ACT.Sigmoid).then_inc(pj_freed, 1)

            def root(j):
                act.wait_ge(var_ready, j + 1)
                nc.scalar.activation(rstd_qk[:, j % 2, :], rstd_qk[:, j % 2, :], ACT.Sqrt).then_inc(qk_rstd, 1)

            def gla_prep():
                act.wait_ge(xy_freed, use(XY_USES, "z"))
                link(nc.scalar.activation(lsp, zb, ACT.Abs))
                link(nc.scalar.activation(lsp, lsp, ACT.Exp, scale=-1.0))
                nc.scalar.activation(lsp, lsp, ACT.Ln, bias=1.0).then_inc(lsp_ready, 1)

            def gla_exps():
                act.wait_ge(decay_ready, 1)
                nc.scalar.activation(q_in, D1, ACT.Exp, scale=1.0 / GATE_NORM)
                nc.scalar.activation(k_in, D1, ACT.Exp, scale=-1.0 / GATE_NORM)
                nc.scalar.activation(q_out, B, ACT.Exp, scale=1.0 / GATE_NORM)
                nc.scalar.activation(k_out, D2, ACT.Exp, scale=-1.0 / GATE_NORM).then_inc(exps_ready, 1)

            def cache_keys():
                act.wait_ge(vw_ready, use(VW_USES, "cache"))
                nc.scalar.copy(ckT.rearrange("p (a b) c -> p a (b c)", a=2), ps[:, VB_:VB_ + 2, :]).then_inc(vw_freed, 1)

            def exps(s):
                act.wait_ge(max_ready, s + 1)
                w0, w1_ = ((P, 256), (P, 256), (0, 256), (0, 256), (0, 192))[s]
                ww = 192 if s == 4 else 256
                for h in range(4):
                    nc.scalar.activation(S_at[:, ww * h + w0:ww * h + w1_], S_at[:, ww * h + w0:ww * h + w1_], ACT.Exp,
                                         bias=small[:, 16 + h:17 + h], accum_out=small[:, 20 + h:21 + h])
                nc.scalar.activation(small[:, 24:28], small[:, 28:32], ACT.Exp).then_inc(exp_done, 1)

            def probs(s):
                act.wait_ge(vw_ready, use(VW_USES, f"probs{s}"))
                if s:
                    act.wait_ge(n_ready, use(N_USES, f"attend{s - 1}"))
                if s < 2:
                    nc.scalar.copy(pT[:, 1, :, :], ps[:, WB, :].rearrange("p (h q) -> p h q", h=4)).then_inc(vw_freed, 1)
                elif s < 4:
                    nc.scalar.copy(pT[:, :, :, :].rearrange("p k h q -> p k (h q)"), ps[:, VB_:VB_ + 2, :]).then_inc(vw_freed, 1)
                else:
                    nc.scalar.copy(pT[:, 0, :, :], ps[:, VB_, :].rearrange("p (h q) -> p h q", h=4))
                    nc.scalar.copy(pT[0:64, 1, :, :], ps[0:64, WB, :].rearrange("p (h q) -> p h q", h=4)).then_inc(vw_freed, 1)

            def gates_early():
                act.wait_ge(pj_freed, tiles_done("ga", 7))
                nc.scalar.activation(rsT[:, :, :], rbT[:, :, :], ACT.Sigmoid).then_inc(gates_ready, 1)
                nc.scalar.activation(gaT[:, :, :], gaT[:, :, :], ACT.Sigmoid).then_inc(gates_ready, 1)

            def gla_prompt_out():
                act.wait_ge(vw_ready, use(VW_USES, "gla_p"))
                act.wait_ge(xy_ready, use(XY_USES, "state3"))
                for j in range(PAIRS):
                    out = nc.scalar.copy(obT[:, 2 * j:2 * j + 2, 0:PROMPT],
                                         ps[:, VB_ + j, :].rearrange("p (a q) -> p a q", a=2))
                out.then_inc(vw_freed, 1)

            def gla_sample_out():
                act.wait_ge(vw_ready, use(VW_USES, "gla_s"))
                for j in range(PAIRS):
                    out = nc.scalar.copy(obT[:, 2 * j:2 * j + 2, PROMPT:T],
                                         ps[:, VB_ + j, 0:P].rearrange("p (a q) -> p a q", a=2))
                out.then_inc(vw_freed, 1)

            for n in range(FIRST_RB):
                evacuate(n)
                if 1 <= n <= 5:
                    root(n - 1)
            after = {
                0: [gla_prep, cache_keys],
                1: [gla_exps],
                2: [lambda: exps(0)],
                4: [lambda: probs(0)],
                5: [lambda: exps(1)],
                6: [lambda: probs(1)],
                7: [lambda: exps(2)],
                8: [lambda: probs(2)],
                9: [lambda: exps(3)],
                10: [lambda: probs(3)],
                11: [lambda: exps(4)],
                12: [lambda: probs(4)],
                14: [gates_early],
                18: [gla_prompt_out],
                19: [gla_sample_out],
            }
            for s in range(20):
                evacuate(FIRST_RB + s)
                for step in after.get(s, ()):
                    step()
            act.wait_ge(vw_freed, use(VW_USES, "gla_s"))
            act.wait_ge(pj_ready, len(TILE_ORDER))
            nc.scalar.activation(squares_o, obT, ACT.Square).then_inc(sqo_ready, 1)
            for h in range(GH):
                act.wait_ge(varo_ready, h + 1)
                nc.scalar.activation(rstd_o[:, h, :], rstd_o[:, h, :], ACT.Sqrt).then_inc(rstdo_ready, 1)
            def squares_h(t):
                r = TILES[t][1]
                act.wait_ge(h_ready, t + 1)
                act.wait_ge(mg_ready, 2 * KD)
                nc.scalar.activation(hn[0:r, t, :], acc[0:r, t, :], ACT.Square,
                                     accum_out=small[0:r, 44 + t:45 + t]).then_inc(ss2_ready, 1)

            def root_h(t):
                r = TILES[t][1]
                act.wait_ge(base2_ready, t + 1)
                nc.scalar.activation(small[0:r, 52 + t:53 + t], small[0:r, 48 + t:49 + t], ACT.Sqrt).then_inc(rstd2_ready, 1)
                act.wait_ge(rstd2_ready, t + 1)
                nc.scalar.activation(hn[0:r, t, :], acc[0:r, t, :], ACT.Copy, scale=small[0:r, 52 + t:53 + t]
                                     ).then_inc(hn_ready, 1)

            def exps_top(t):
                r = TILES[t][1]
                act.wait_ge(top_ready, t + 1)
                nc.scalar.activation(top_e[t][0:r, :], top8[t][0:r, 0:4], ACT.Exp, bias=top_neg[t][0:r, :],
                                     accum_out=top_sum[t][0:r, :]).then_inc(gexp_ready, 1)

            for t in range(3):
                squares_h(t)
                root_h(t)
            for t in range(3):
                exps_top(t)

            def copy_u(n, first=False):
                act.wait_ge(w1_used, KD * n + KD)
                if not first:
                    act.wait_ge(ut_done, n)
                nc.scalar.copy(u_sb[:, :, :], ps[:, 0:2, :]).then_inc(u_copied, 1)

            def gate_sigmoid(n, first=False):
                act.wait_ge(glu_ready, n + 1)
                if not first:
                    act.wait_ge(h_act, n)
                nc.scalar.activation(sig, glu, ACT.Sigmoid, scale=1.702).then_inc(sig_ready, 1)

            def copy_y(n, which, combined):
                act.wait_ge(w2_used, 4 * n + 4)
                act.wait_ge(comb_done, combined)
                nc.scalar.copy(y_sb[:, which, :], ps[:, 6, :]).then_inc(y_copied, 1)

            def copy_gates(p):
                for which in range(2):
                    act.wait_ge(gpT_done, 2 * p + which + 1)
                    act.wait_ge(comb_done, 3 * p + 3)
                    nc.scalar.copy(gpickT[:, which, 0:T], ps[:, 7, 0:T]).then_inc(gpT_copied, 1)

            def body(p, first=False, main=False):
                copy_u(2 * p, first=first and main)
                if not first:
                    copy_y(2 * p - 1, 1, 3 * p)
                elif main:
                    act.wait_ge(gT_psum, 1)
                    nc.scalar.copy(gateT[:, :], ps[0:EXPERTS, 6, 0:T]).then_inc(gT_copied, 1)
                gate_sigmoid(2 * p, first=first and main)
                copy_u(2 * p + 1)
                copy_y(2 * p, 0, 3 * p + 3)
                copy_gates(p)
                gate_sigmoid(2 * p + 1)

            def last_body(p):
                copy_u(2 * p)
                gate_sigmoid(2 * p)
                copy_y(2 * p - 1, 1, 3 * p)
                copy_gates(p)
                copy_y(2 * p, 0, 3 * p + 3)
                copy_u(2 * p + 1)
                gate_sigmoid(2 * p + 1)
                copy_y(2 * p + 1, 1, 3 * p + 3)

            HALF = EXPERTS // 2
            body(0, first=True, main=True)
            with act.Fori(1, HALF - 1) as i:
                body(i)
            last_body(HALF - 1)
            act.wait_ge(count_ready, 1)
            busiest = act.value_load(most[0:1, 0:1], min_val=0, max_val=T)
            with act.If(busiest > SLOTS):
                with act.Fori(1, PASSES) as b:
                    body(HALF * b, first=True)
                    with act.Fori(1, HALF - 1) as i:
                        body(HALF * b + i)
                    last_body(HALF * b + HALF - 1)
                act.nop()
            act.nop()

        @block.vector
        def _(dve):
            steps = [0]

            def link(ins):
                steps[0] += 1
                ins.then_inc(dve_steps, 1)
                dve.wait_ge(dve_steps, steps[0])

            def wide(ap, shape):
                return ap.broadcast_to(shape)

            for t, (_, r) in enumerate(TILES):
                dve.wait_ge(ss_ready, t + 1)
                link(dve.tensor_scalar(small[0:r, 4 + t:5 + t], small[0:r, t:t + 1], 1.0 / D, NORM_EPS, ALU.mult, ALU.add))
                dve.reciprocal(small[0:r, 4 + t:5 + t], small[0:r, 4 + t:5 + t]).then_inc(rstd_base, 1)
            for t, (_, r) in enumerate(TILES):
                dve.wait_ge(rstd_ready, t + 1)
                dve.tensor_scalar(xn[0:r, t, :], acc[0:r, t, :], small[0:r, 8 + t:9 + t], None, ALU.mult
                                  ).then_inc(xn_ready, 1)
            dve.wait_ge(n_ready, use(N_USES, "n1_column"))
            dve.tensor_copy(cols[:, 0:8], ps[:, NB, 0:8]).then_inc(n_freed, 1)
            dve.wait_ge(n_freed, use(N_USES, "n1_column"))
            for t, (t0, r) in enumerate(TILES):
                for half in range(2):
                    u = 2 * t + half
                    dve.wait_ge(xT_ready, u + 1)
                    dve.tensor_tensor(xnT[:, 4 * half:4 * half + 4, t0:t0 + r],
                                      ps[:, XB + u % 4, :].rearrange("p (k q) -> p k q", k=4)[:, :, 0:r],
                                      wide(cols[:, 4 * half:4 * half + 4].unsqueeze(2), [P, 4, r]), ALU.mult
                                      ).then_inc(xnT_ready, 1)
            dve.wait_ge(n_ready, use(N_USES, "vectors"))
            dve.tensor_copy(cols[:, 8:21], ps[:, NB, 0:13]).then_inc(n_freed, 1)
            dve.wait_ge(n_freed, use(N_USES, "vectors"))
            for j in range(5):
                b = j % 2
                dve.wait_ge(n_ready, use(N_USES, f"norm{j}"))
                if j >= 2:
                    dve.wait_ge(qk_done, j - 1)
                dve.tensor_scalar(rstd_qk[:, b, :], ps[:, NB, 0:T], QK_EPS, None, ALU.add).then_inc(n_freed, 1)
                dve.wait_ge(n_freed, use(N_USES, f"norm{j}"))
                dve.reciprocal(rstd_qk[:, b, :], rstd_qk[:, b, :]).then_inc(var_ready, 1)
                dve.wait_ge(qk_rstd, j + 1)
                dve.wait_ge(pj_freed, j + 1)
                if j < 4:
                    dve.scalar_tensor_tensor(qT[:, j, :], raw[:, b, 0:PROMPT], cols[:, 18:19], rstd_qk[:, b, 0:PROMPT],
                                             ALU.mult, ALU.mult)
                    dve.scalar_tensor_tensor(qS[:, :, j, :], raw[:, b, PROMPT:T].rearrange("p (b t) -> p b t", t=TSEQ),
                                             cols[:, 18:19], rstd_qk[:, b, PROMPT:T].rearrange("p (b t) -> p b t", t=TSEQ),
                                             ALU.mult, ALU.mult).then_inc(qk_done, 1)
                else:
                    dve.scalar_tensor_tensor(kT[:, :], raw[:, b, :], cols[:, 19:20], rstd_qk[:, b, :],
                                             ALU.mult, ALU.mult).then_inc(qk_done, 1)

            dve.wait_ge(n_ready, use(N_USES, "b1"))
            dve.tensor_copy(b1T[:, :, :, :].rearrange("p e g f -> p (g f) e"),
                            ps[:, NB, :].rearrange("p (c e) -> p c e", e=EXPERTS)).then_inc(n_freed, 1)
            dve.wait_ge(small_in, 16 * 6)
            dve.wait_ge(consts_in, 16)
            for i in range(2):
                dve.tensor_copy(sinkr[:, i, :].rearrange("p (g j) -> p g j", g=KVH),
                                sinkc[:, :].rearrange("p (g h) -> p g h", g=KVH)[:, :, 2 * i:2 * i + 2])
            link(dve.tensor_tensor(sink_s[:, :, :], sinkc[:, :].rearrange("p (g h) -> p g h", g=KVH),
                                   wide(const("head_of").unsqueeze(1), [P, KVH, GROUP]), ALU.mult))
            link(dve.tensor_reduce(small[:, 36:38], sink_s[:, :, :], AX.X, ALU.add))
            link(dve.tensor_copy(sinkr[:, 2, :].rearrange("p (g h) -> p g h", g=KVH),
                                 wide(small[:, 36:38].unsqueeze(2), [P, KVH, 2])))

            dve.wait_ge(xy_ready, use(XY_USES, "z"))
            for j in range(PAIRS):
                last = dve.tensor_scalar(zb[:, j, :], ps[:, XB + j, 0:T], cols[:, 16 + j:17 + j], None, ALU.add)
            last.then_inc(xy_freed, 1)
            dve.wait_ge(xy_freed, use(XY_USES, "z"))
            dve.wait_ge(lsp_ready, 1)
            link(dve.scalar_tensor_tensor(zb, zb, 0.0, lsp, ALU.min, ALU.subtract))
            for j in range(PAIRS):
                scan = dve.tensor_tensor_scan(B[:, j, :], const("keep"), zb[:, j, :], 0.0, ALU.mult, ALU.add)
            link(scan)
            for first, end, c in ((0, PROMPT, CHUNK), (PROMPT, T, TSEQ)):
                b4 = B[:, :, first:end].rearrange("p j (n c) -> p j n c", c=c)
                shape = [P, PAIRS, (end - first) // c, c]
                for dst, at in ((D1, c // 2 - 1), (D2, c - 1)):
                    last = dve.tensor_tensor(dst[:, :, first:end].rearrange("p j (n c) -> p j n c", c=c), b4,
                                             wide(b4[:, :, :, at:at + 1], shape), ALU.subtract)
            last.then_inc(decay_ready, 1)

            dve.wait_ge(n_ready, use(N_USES, "keys"))
            dve.tensor_copy(kTok[:, 0, :], ps[:, NB, 0:P])
            dve.tensor_copy(kTok[0:64, 1, :], ps[0:64, NB, P:2 * P]).then_inc(n_freed, 1)


            def softmax_max(s):
                dve.wait_ge(xy_ready, use(XY_USES, f"scores{s}"))
                if s:
                    dve.wait_ge(vw_ready, use(VW_USES, f"probs{s - 1}"))
                for g in range(KVH):
                    bank = ps[:, XB + g, :]
                    if s < 4:
                        w = 256 if s >= 2 else P
                        out = S_at[:, 512 * g:512 * g + 512].rearrange("p (h c) -> p h c", h=2)[:, :, 256 - w:256]
                        last = dve.scalar_tensor_tensor(
                            out, bank.rearrange("p (h c) -> p h c", h=2)[:, :, 0:w], SCALE,
                            wide(const("band")[:, 256 - w:256].unsqueeze(1), [P, 2, w]), ALU.mult, ALU.add)
                    else:
                        last = dve.scalar_tensor_tensor(S_at[:, 384 * g:384 * g + 384], bank[:, 0:384], SCALE,
                                                        const("sample_mask"), ALU.mult, ALU.add)
                last.then_inc(xy_freed, 1)
                dve.wait_ge(xy_freed, use(XY_USES, f"scores{s}"))
                all_s = probs_of(s)
                sink = sinkr[:, 2 if s == 4 else s % 2, :]
                link(dve.tensor_reduce(small[:, 12:16], all_s, AX.X, ALU.max))
                link(dve.tensor_tensor(small[:, 12:16], small[:, 12:16], sink, ALU.max))
                dve.tensor_scalar(small[:, 16:20], small[:, 12:16], -1.0, None, ALU.mult)
                dve.tensor_tensor(small[:, 28:32], sink, small[:, 12:16], ALU.subtract).then_inc(max_ready, 1)

            def probs_of(s):
                if s == 4:
                    return S_at[:, 0:768].rearrange("p (h c) -> p h c", h=4)
                return S_at.rearrange("p (h c) -> p h c", h=4)[:, :, (0 if s >= 2 else P):256]

            def softmax_norm(s):
                dve.wait_ge(exp_done, s + 1)
                all_s = probs_of(s)
                w = (P, P, 256, 256, 192)[s]
                link(dve.tensor_tensor(small[:, 20:24], small[:, 20:24], small[:, 24:28], ALU.add))
                link(dve.reciprocal(small[:, 32:36], small[:, 20:24]))
                dve.tensor_tensor(all_s, all_s, wide(small[:, 32:36].unsqueeze(2), [P, 4, w]), ALU.mult
                                  ).then_inc(p_ready, 1)

            def attended(s):
                dve.wait_ge(n_ready, use(N_USES, f"attend{s}"))
                if s < 4:
                    n, i = divmod(s, 2)
                    dve.tensor_copy(oT[:, 2 * i:2 * i + 2, P * n:P * n + P],
                                    ps[:, NB, 0:256].rearrange("p (j q) -> p j q", j=2)).then_inc(n_freed, 1)
                else:
                    dve.tensor_copy(oT[:, :, PROMPT:T].rearrange("p j (b t) -> p b j t", t=TSEQ),
                                    ps[:, NB, 0:256].rearrange("p (b j t) -> p b j t", b=NSEQ, j=4)).then_inc(n_freed, 1)

            def mask_decays_prompt():
                dve.wait_ge(xy_ready, use(XY_USES, "decays_p"))
                for a in range(2):
                    last = dve.tensor_tensor(AT_p[:, a, :, :, :].rearrange("p t j s -> p (t j) s"),
                                             ps[:, XB + a, :].rearrange("p (c s) -> p c s", c=4),
                                             wide(const("gla_mask").unsqueeze(1), [P, 4, P]), ALU.mult)
                last.then_inc(xy_freed, 1)

            def mask_decays_sample():
                dve.memset(AT_s[64:128, :, :, :], 0.0)
                dve.wait_ge(xy_ready, use(XY_USES, "decays_s"))
                for a in range(2):
                    last = dve.tensor_tensor(AT_s[0:64, a, :, :],
                                             ps[0:64, XB + a, 0:P].rearrange("p (c s) -> p c s", c=2),
                                             wide(const("gla_smask", 64).unsqueeze(1), [64, 2, 64]), ALU.mult)
                last.then_inc(xy_freed, 1)

            def mask_keys(t):
                dve.wait_ge(n_ready, use(N_USES, f"gkeys{t}"))
                if t == 1:
                    dve.wait_ge(xy_ready, use(XY_USES, "state0"))
                r = TILES[t][1]
                count, dst, which = ((CPT, kM, "chunk_of"), (NSEQ, kMs[0:64, :, :], "seq_of"))[t == 2]
                dve.tensor_tensor(dst, wide(ps[0:r, NB, 0:256].unsqueeze(1), [r, count, 256]),
                                  wide(const(which, r).unsqueeze(2), [r, count, 256]), ALU.mult).then_inc(n_freed, 1)

            def step_states(which):
                dve.wait_ge(xy_ready, use(XY_USES, f"state{which}"))
                if which == 2:
                    dve.wait_ge(s0_in, 16)
                for c in range(4):
                    for j in range(PAIRS):
                        update = ps[:, XB + c // 2, 256 * (c % 2) + P * j:256 * (c % 2) + P * j + P]
                        if which < 2:
                            n = 4 * which + c
                            if n == 0:
                                last = dve.tensor_copy(S_all[:, 1, j, :], update)
                            else:
                                last = dve.scalar_tensor_tensor(S_all[:, n + 1, j, :], S_all[:, n, j, :],
                                                                dec[:, j, n:n + 1], update, ALU.mult, ALU.add)
                        else:
                            b = 4 * (which - 2) + c
                            last = dve.scalar_tensor_tensor(S_new[:, b, j, :], S0[:, b, j, :],
                                                            dec[:, j, NCH + b:NCH + b + 1], update, ALU.mult, ALU.add)
                    if which < 2 and c < 3:
                        link(last)
                last.then_inc(xy_freed, 1)
                if which == 0:
                    dve.wait_ge(xy_freed, use(XY_USES, "state0"))

            def gla_operands():
                dve.wait_ge(exps_ready, 1)
                dve.tensor_copy(dec[:, :, 0:NCH], q_out[:, :, CHUNK - 1:PROMPT:CHUNK])
                link(dve.tensor_copy(dec[:, :, NCH:], q_out[:, :, PROMPT + TSEQ - 1:T:TSEQ]))
                dve.tensor_tensor(q_in, q_in, qbT[:, :, :], ALU.mult)
                dve.tensor_tensor(k_in, k_in, kbT[:, :, :], ALU.mult)
                for a in range(2):
                    r0, o0 = 64 * a, 64 * (1 - a)
                    dve.memset(q_pair[o0:o0 + 64, a, :, :], 0.0)
                    dve.tensor_tensor(q_pair[r0:r0 + 64, a, :, :], q_out[r0:r0 + 64, :, :], qbT[r0:r0 + 64, :, :], ALU.mult)
                dve.tensor_tensor(k_out, k_out, kbT[:, :, :], ALU.mult).then_inc(gla_ops, 1)

            softmax_max(0)
            for s in range(4):
                softmax_norm(s)
                softmax_max(s + 1)
                if s == 0:
                    gla_operands()
                attended(s)
            softmax_norm(4)
            mask_decays_prompt()
            attended(4)
            mask_decays_sample()
            mask_keys(0)
            step_states(0)
            mask_keys(1)
            step_states(1)
            mask_keys(2)
            step_states(2)
            dve.wait_ge(gates_ready, 2)
            step_states(3)
            link(dve.tensor_tensor(rbT[:, :, :], rbT[:, :, :], rsT[:, :, :], ALU.mult))
            dve.wait_ge(pj_freed, tiles_done("gb", 7))

            def merge_a(m):
                dve.wait_ge(mg_ready, m + 1)
                dve.tensor_tensor(gaT[:, m, :], gaT[:, m, :], ps[:, m % 3, 0:T], ALU.mult).then_inc(mg_freed, 1)

            dve.wait_ge(sqo_ready, 1)
            link(dve.scalar_tensor_tensor(obT, obT, cols[:, 20:21], rbT[:, :, :], ALU.mult, ALU.mult))
            def scale_out(h):
                dve.wait_ge(rstdo_ready, h + 1)
                dve.tensor_tensor(obT[:, h, :], obT[:, h, :], rstd_o[:, h, :], ALU.mult).then_inc(ob_done, 1)

            merge_a(0)
            for h in range(GH):
                merge_a(h + 1)
                dve.wait_ge(n_ready, use(N_USES, f"dv{h}"))
                dve.tensor_scalar(rstd_o[:, h, :], ps[:, NB, 0:T], NORM_EPS, None, ALU.add).then_inc(n_freed, 1)
                dve.wait_ge(n_freed, use(N_USES, f"dv{h}"))
                dve.reciprocal(rstd_o[:, h, :], rstd_o[:, h, :]).then_inc(varo_ready, 1)
                if h:
                    scale_out(h - 1)
            merge_a(GH + 1)
            scale_out(GH - 1)
            for m in range(GH + 2, KD):
                merge_a(m)
            for m in range(KD):
                u = KD + m
                dve.wait_ge(mg_ready, u + 1)
                dve.tensor_tensor(gbT[:, m, :], gbT[:, m, :], ps[:, u % 3, 0:T], ALU.mult).then_inc(mg_freed, 1)
                dve.wait_ge(mg_freed, u + 1)
                dve.tensor_tensor(xnT[:, m, :], gaT[:, m, :], gbT[:, m, :], ALU.add).then_inc(merged_ready, 1)
            def add_h(t):
                r = TILES[t][1]
                bank = (XB, VB_, XB)[t]
                dve.wait_ge(h_psum, t + 1)
                if t < 2:
                    dve.tensor_tensor(acc[:, t, :], acc[:, t, :],
                                      ps[:, bank:bank + 2, :].rearrange("p a b -> p (a b)"), ALU.add).then_inc(h_ready, 1)
                else:
                    dve.tensor_tensor(acc[0:64, t, 0:512], acc[0:64, t, 0:512], ps[0:64, bank, :], ALU.add)
                    dve.tensor_tensor(acc[0:64, t, 512:D], acc[0:64, t, 512:D], ps[64:128, bank, :], ALU.add
                                      ).then_inc(h_ready, 1)

            def turned_h(t):
                t0, r = TILES[t]
                bank = (0, VB_, 0)[t]
                dve.wait_ge(hnT_psum, t + 1)
                dve.tensor_tensor(hnT[:, :, t0:t0 + r],
                                  ps[:, bank:bank + 2, :].rearrange("p a (k q) -> p (a k) q", k=4)[:, :, 0:r],
                                  wide(cols[:, 8:16].unsqueeze(2), [P, KD, r]), ALU.mult).then_inc(hnT_ready, 1)

            def rms_h(t):
                r = TILES[t][1]
                dve.wait_ge(ss2_ready, t + 1)
                link(dve.tensor_scalar(small[0:r, 48 + t:49 + t], small[0:r, 44 + t:45 + t], 1.0 / D, NORM_EPS,
                                       ALU.mult, ALU.add))
                dve.reciprocal(small[0:r, 48 + t:49 + t], small[0:r, 48 + t:49 + t]).then_inc(base2_ready, 1)

            def choose(t):
                r = TILES[t][1]
                dve.wait_ge(lg_psum, t + 1)
                dve.wait_ge(rstd2_ready, t + 1)
                dve.scalar_tensor_tensor(lg[t][0:r, :], ps[0:r, 2, 0:EXPERTS], small[0:r, 52 + t:53 + t], b_rt[0:r, :],
                                         ALU.mult, ALU.add).then_inc(lgt_freed, 1)
                dve.wait_ge(lgt_freed, t + 1)
                link(dve.max(top8[t][0:r, :], lg[t][0:r, :]))
                link(dve.max_index(idx8[0:r, t, :], top8[t][0:r, :], lg[t][0:r, :]))
                link(dve.tensor_copy(idxf[t][0:r, :], idx8[0:r, t, 0:4]))
                link(dve.tensor_tensor(onehot[t][0:r, :, :], wide(const("expert", r).unsqueeze(1), [r, TOPK, EXPERTS]),
                                       wide(idxf[t][0:r, :].unsqueeze(2), [r, TOPK, EXPERTS]), ALU.is_equal))
                dve.tensor_reduce(sel[0:r, t, :], onehot[t][0:r, :, :].rearrange("p k e -> p e k"), AX.X, ALU.add
                                  ).then_inc(sel_ready, 1)
                dve.tensor_scalar(top_neg[t][0:r, :], top8[t][0:r, 0:1], -1.0, None, ALU.mult).then_inc(top_ready, 1)

            def weigh():
                rows_ = [r for _, r in TILES]
                dve.wait_ge(gexp_ready, 3)
                for t, r in enumerate(rows_):
                    last = dve.reciprocal(top_inv[t][0:r, :], top_sum[t][0:r, :])
                link(last)
                for t, r in enumerate(rows_):
                    last = dve.tensor_scalar(top_e[t][0:r, :], top_e[t][0:r, :], top_inv[t][0:r, :], None, ALU.mult)
                link(last)
                for t, r in enumerate(rows_):
                    last = dve.tensor_tensor(onehot_g[t][0:r, :, :], onehot[t][0:r, :, :],
                                             wide(top_e[t][0:r, :].unsqueeze(2), [r, TOPK, EXPERTS]), ALU.mult)
                link(last)
                for t, r in enumerate(rows_):
                    last = dve.tensor_reduce(gates[0:r, t, 0:EXPERTS], onehot_g[t][0:r, :, :].rearrange("p k e -> p e k"),
                                             AX.X, ALU.add)
                last.then_inc(route_ready, 1)

            def placed():
                dve.wait_ge(pos_psum, 4)
                dve.wait_ge(sel_ready, 3)
                for r, a, b in ((P, 0, 2), (64, 2, 3)):
                    last = dve.scalar_tensor_tensor(
                        place[0:r, a:b, 0:EXPERTS],
                        ps[0:r, NB, EXPERTS * a:EXPERTS * b].rearrange("p (t e) -> p t e", e=EXPERTS), 1.0,
                        sel[0:r, a:b, :], ALU.add, ALU.mult)
                link(last)

            for t in range(3):
                dve.wait_ge(x_again[t], 16)
            dve.wait_ge(pads_ready, 4)
            dve.wait_ge(small_in, 16 * 6)
            add_h(0)
            turned_h(0)
            rms_h(0)
            add_h(1)
            rms_h(1)
            add_h(2)
            turned_h(1)
            turned_h(2)
            rms_h(2)
            for t in range(3):
                choose(t)
            placed()

            def count():
                link(dve.tensor_reduce(small[0:1, 60:61], ps[0:1, NB, 96:128], AX.X, ALU.max))
                dve.tensor_copy(most[:, :], small[0:1, 60:61]).then_inc(count_ready, 1)

            def pick_tokens(p, e, fresh=False):
                if not fresh:
                    dve.wait_ge(gather_done, 2 * p)
                for which in range(2):
                    for t, (_, r) in enumerate(TILES):
                        last = dve.tensor_scalar(pick[0:r, t, SLOTS * which:SLOTS * (which + 1)],
                                                 const("slot", r)[:, 0:SLOTS], place[0:r, t, bass.ds(e + which, 1)], None,
                                                 ALU.is_equal)
                last.then_inc(pick_ready, 1)

            def pick_gates(p, e, fresh=False):
                if not fresh:
                    dve.wait_ge(gpT_done, 2 * p)
                for which in range(2):
                    for t, (_, r) in enumerate(TILES):
                        last = dve.tensor_scalar(gpick[0:r, t, which, :], const("slot", r),
                                                 place[0:r, t, bass.ds(e + which, 1)],
                                                 gates[0:r, t, bass.ds(e + which, 1)], ALU.is_equal, ALU.mult)
                last.then_inc(gpick_ready, 1)

            def take_tokens(p, fresh=False):
                if not fresh:
                    dve.wait_ge(w1_used, 2 * KD * p)
                for half in range(2):
                    dve.wait_ge(gather_done, 2 * p + half + 1)
                    dve.tensor_tensor(xeT[:, 4 * half:4 * half + 4, :], ps[:, 7 - half if fresh else 7, :].rearrange("p (k s) -> p k s", k=4),
                                      wide(cols[:, 8 + 4 * half:12 + 4 * half].unsqueeze(2), [P, 4, P]), ALU.mult
                                      ).then_inc(xe_ready, 1)

            def swiglu(n, e, which, fresh=False):
                dve.wait_ge(ut_done, n + 1)
                if not fresh:
                    dve.wait_ge(h_act, n)
                dve.tensor_tensor(glu, ps[:, 2, :].rearrange("p (f t) -> p f t", f=KF),
                                  wide(b1T[:, bass.ds(e, 1), 0, :].rearrange("p a f -> p (a f)").unsqueeze(2), [P, KF, SLOTS]),
                                  ALU.add).then_inc(glu_biased, 1)
                dve.wait_ge(glu_biased, n + 1)
                dve.tensor_scalar(glu, glu, 7.0, None, ALU.min).then_inc(glu_ready, 1)
                dve.tensor_tensor(lin, ps[:, 3, :].rearrange("p (f t) -> p f t", f=KF),
                                  wide(b1T[:, bass.ds(e, 1), 1, :].rearrange("p a f -> p (a f)").unsqueeze(2), [P, KF, SLOTS]),
                                  ALU.add).then_inc(lin_biased, 1)
                dve.wait_ge(lin_biased, n + 1)
                dve.tensor_scalar(lin, lin, 7.0, -7.0, ALU.min, ALU.max).then_inc(lin_ready, 1)
                dve.wait_ge(lin_ready, n + 1)
                dve.scalar_tensor_tensor(lin, lin, 1.0, glu, ALU.add, ALU.mult).then_inc(prod_ready, 1)
                dve.wait_ge(prod_ready, n + 1)
                dve.wait_ge(sig_ready, n + 1)
                if not fresh:
                    dve.wait_ge(w2_used, 4 * (n - 1))
                dve.tensor_tensor(hT[:, which, :, :], lin, sig, ALU.mult).then_inc(h_act, 1)

            def add(c, t, bank=XB):
                r = TILES[t][1]
                dve.wait_ge(comb_done, c + 1)
                dve.tensor_tensor(acc[0:r, t, :], acc[0:r, t, :],
                                  ps[0:r, bank:bank + 2, :].rearrange("p a b -> p (a b)"), ALU.add).then_inc(comb_added, 1)

            def body(p, i, first=False, main=False, last=False):
                fresh = first and main
                if first:
                    take_tokens(p, fresh)
                if fresh:
                    weigh()
                    count()
                pick_gates(p, 2 * i, fresh)
                if not last:
                    pick_tokens(p + 1, 2 * i + 2)
                swiglu(2 * p, 2 * i, 0, fresh)
                if not first or main:
                    for t in range(3):
                        add(3 * p + t, t, (XB, 0 if last else XB, 2)[t])
                if not last:
                    take_tokens(p + 1)
                swiglu(2 * p + 1, 2 * i + 1, 1)

            def tail(p):
                for t in range(3):
                    add(3 * p + t, t, (XB, 0, 2)[t])

            HALF = EXPERTS // 2
            pick_tokens(0, 0, fresh=True)
            dve.memset(gpickT[:, :, T:], 0.0)
            body(0, 0, first=True, main=True)
            with dve.Fori(1, HALF - 1) as i:
                body(i, i)
            body(HALF - 1, HALF - 1, last=True)
            tail(HALF)
            busiest = dve.value_load(most[0:1, 0:1], min_val=0, max_val=T)
            with dve.If(busiest > SLOTS):
                with dve.Fori(1, PASSES) as b:
                    dve.tensor_scalar(const("slot"), const("slot"), float(SLOTS), None, ALU.add).then_inc(slots_moved, 1)
                    dve.wait_ge(slots_moved, b)
                    pick_tokens(HALF * b, 0)
                    body(HALF * b, 0, first=True)
                    with dve.Fori(1, HALF - 1) as i:
                        body(HALF * b + i, i)
                    body(HALF * b + HALF - 1, HALF - 1, last=True)
                    tail(HALF * b + HALF)


_INS = ["x_prompt", "x_sample", "cache_swa_k", "cache_swa_v", "state_gla", "norm1", "w_in", "q_norm", "k_norm",
        "sinks", "w_gk", "b_gk", "gla_norm", "w_a", "w_b", "w_o", "norm2", "w_router", "b_router", "w1", "b1",
        "w2", "b2"]
_OUTS = [(1, 256, 1024), (8, 8, 1024), (1, 1, 128, 2, 64), (1, 1, 128, 2, 64), (1, 1, 4, 64, 128),
         (1, 8, 128, 2, 64), (1, 8, 128, 2, 64), (1, 8, 4, 64, 128)]


def kernel(**inputs):
    import concourse.bacc as bacc
    from concourse.bass_utils import run_bass_kernel_spmd

    nc = bacc.Bacc("TRN2", target_bir_lowering=False, num_devices=1)
    arrays, args = {}, []
    for name in _INS + ["consts"]:
        a = constants() if name == "consts" else np.ascontiguousarray(inputs[name])
        arrays[f"in_{name}"] = a
        args.append(nc.dram_tensor(f"in_{name}", a.shape, mybir.dt.from_np(a.dtype), kind="ExternalInput").ap())
    for i, shape in enumerate(_OUTS):
        args.append(nc.dram_tensor(f"out_{i}", shape, F32, kind="ExternalOutput").ap())
    layer(nc, *args)
    r = run_bass_kernel_spmd(nc, [arrays], core_ids=[0])
    return tuple(r.results[0][f"out_{i}"] for i in range(len(_OUTS)))
```
